# Optimizing a Trainium2 kernel written in Bass

```python
import jax, jax.numpy as jnp
from jax import lax
import numpy as np

D_MODEL = 2048
BATCH = 1
SEQ = 512
DEPTH = 1
DEC_BATCH = 8
DEC_SEQ = 1
PAST_LEN = 1024
PAGE_SIZE = 128

MIX_WIDTH = D_MODEL
C_CONV = MIX_WIDTH // 2
N_HEADS = 8
HEAD_DIM = (MIX_WIDTH - C_CONV) // N_HEADS
ATTN_W = N_HEADS * HEAD_DIM
CONV_W = 31
N_IDX_HEADS = 16
D_IDX = 64
TOPK_MAX = 256
D_FF = 4 * D_MODEL
ROPE_THETA = 10000.0
EPS = 1e-6
Q_BLOCK = 128

IN_SPLITS = (C_CONV, 2 * C_CONV, 2 * C_CONV + ATTN_W, 2 * C_CONV + 2 * ATTN_W,
             2 * C_CONV + 3 * ATTN_W, 2 * C_CONV + 3 * ATTN_W + N_IDX_HEADS * D_IDX,
             2 * C_CONV + 3 * ATTN_W + N_IDX_HEADS * D_IDX + D_IDX)
D_IN = 2 * C_CONV + 3 * ATTN_W + N_IDX_HEADS * D_IDX + D_IDX + N_IDX_HEADS

kernel_name = 'hymba_conformer_dsa_step'

F32 = jnp.float32

def rms_norm(x, g):
    xf = x.astype(F32)
    y = xf * lax.rsqrt(jnp.mean(xf * xf, axis=-1, keepdims=True) + EPS)
    return (y * g.astype(F32)).astype(x.dtype)

def layer_norm(x, g, b):
    xf = x.astype(F32)
    mu = jnp.mean(xf, axis=-1, keepdims=True)
    var = jnp.mean(jnp.square(xf - mu), axis=-1, keepdims=True)
    return ((xf - mu) * lax.rsqrt(var + EPS) * g.astype(F32) + b.astype(F32)).astype(x.dtype)

def rope(x, pos):
    half = x.shape[-1] // 2
    inv_freq = ROPE_THETA ** (-jnp.arange(half, dtype=F32) / half)
    ang = pos.astype(F32)[:, None] * inv_freq[None, :]
    cos = jnp.cos(ang)[None, :, None, :]
    sin = jnp.sin(ang)[None, :, None, :]
    xf = x.astype(F32)
    x1, x2 = xf[..., :half], xf[..., half:]
    return jnp.concatenate([x1 * cos - x2 * sin, x2 * cos + x1 * sin], axis=-1).astype(x.dtype)

def causal_depthwise_conv(u_ext, conv_w, conv_b):
    y = lax.conv_general_dilated(u_ext, conv_w[:, None, :].astype(u_ext.dtype), window_strides=(1,),
                                 padding='VALID', dimension_numbers=('NWC', 'WIO', 'NWC'),
                                 feature_group_count=u_ext.shape[-1])
    return y + conv_b.astype(y.dtype)

def index_scores(qi, ki, wi):
    dots = jnp.einsum('nqhd,nsd->nqhs', qi, ki).astype(F32) * (D_IDX ** -0.5)
    return jnp.einsum('nqh,nqhs->nqs', wi.astype(F32) * (N_IDX_HEADS ** -0.5), jax.nn.relu(dots))

def attend_gathered(q, kg, vg, ok):
    s = jnp.einsum('nqhd,nqkhd->nqhk', q, kg).astype(F32) * (HEAD_DIM ** -0.5)
    s = jnp.where(ok[:, :, None, :], s, -jnp.inf)
    p = jax.nn.softmax(s, axis=-1).astype(vg.dtype)
    return jnp.einsum('nqhk,nqkhd->nqhd', p, vg)

def sparse_attend_prompt(q, k, v, qi, ki, wi):
    nb, t = q.shape[:2]
    topk = min(TOPK_MAX, t // 4)
    spos = jnp.arange(t)
    bidx = jnp.arange(nb)[:, None, None]

    def block(start):
        qb = lax.dynamic_slice_in_dim(q, start, Q_BLOCK, axis=1)
        qib = lax.dynamic_slice_in_dim(qi, start, Q_BLOCK, axis=1)
        wib = lax.dynamic_slice_in_dim(wi, start, Q_BLOCK, axis=1)
        tpos = start + jnp.arange(Q_BLOCK)
        allowed = spos[None, :] <= tpos[:, None]
        scores = jnp.where(allowed[None], index_scores(qib, ki, wib), -jnp.inf)
        _, idx = lax.top_k(scores, topk)
        ok = idx <= tpos[None, :, None]
        return attend_gathered(qb, k[bidx, idx], v[bidx, idx], ok)

    out = lax.map(block, jnp.arange(0, t, Q_BLOCK))
    return jnp.moveaxis(out, 0, 1).reshape(nb, t, N_HEADS, HEAD_DIM)

def sparse_attend_sample(q, k, v, qi, ki, wi, cache_k, cache_v, cache_kidx, page_table, layer):
    nb, t_new = q.shape[:2]
    past = page_table.shape[1] * PAGE_SIZE
    n_keys = past + t_new
    topk = min(TOPK_MAX, n_keys // 4)
    ki_past = cache_kidx[layer, page_table].reshape(nb, past, D_IDX).astype(ki.dtype)
    ki_all = jnp.concatenate([ki_past, ki], axis=1)
    tpos = past + jnp.arange(t_new)
    allowed = jnp.arange(n_keys)[None, :] <= tpos[:, None]
    scores = jnp.where(allowed[None], index_scores(qi, ki_all, wi), -jnp.inf)
    _, idx = lax.top_k(scores, topk)
    ok = idx <= tpos[None, :, None]
    bidx = jnp.arange(nb)[:, None, None]
    pidx = jnp.minimum(idx, past - 1)
    phys = page_table[bidx, pidx // PAGE_SIZE]
    off = pidx % PAGE_SIZE
    nidx = jnp.clip(idx - past, 0, t_new - 1)
    from_past = (idx < past)[..., None, None]
    kg = jnp.where(from_past, cache_k[layer, phys, off].astype(k.dtype), k[bidx, nidx])
    vg = jnp.where(from_past, cache_v[layer, phys, off].astype(v.dtype), v[bidx, nidx])
    return attend_gathered(q, kg, vg, ok)

def hybrid_layer(x, c, pos, conv_prev, attend_fn, norm1_g, w_ada, b_ada, w_in, conv_w, conv_b,
                 conv_ln_g, conv_ln_b, w_out, norm2_g, w_ff1, w_ff2):
    nb, t, _ = x.shape
    mod = (jax.nn.silu(c) @ w_ada + b_ada)[:, None, :]
    shift1, scale1, gate1, shift2, scale2, gate2 = jnp.split(mod, 6, axis=-1)
    h = rms_norm(x, norm1_g) * (1 + scale1) + shift1
    u_a, u_g, q, k, v, qi, ki, wi = jnp.split(h @ w_in, IN_SPLITS, axis=-1)
    u = u_a * jax.nn.sigmoid(u_g)
    u_ext = jnp.concatenate([conv_prev.astype(u.dtype), u], axis=1)
    a_out = jax.nn.silu(layer_norm(causal_depthwise_conv(u_ext, conv_w, conv_b), conv_ln_g, conv_ln_b))
    q = rope(q.reshape(nb, t, N_HEADS, HEAD_DIM), pos)
    k = rope(k.reshape(nb, t, N_HEADS, HEAD_DIM), pos)
    v = v.reshape(nb, t, N_HEADS, HEAD_DIM)
    qi = rope(qi.reshape(nb, t, N_IDX_HEADS, D_IDX), pos)
    ki = rope(ki[:, :, None, :], pos)[:, :, 0, :]
    b_out = attend_fn(q, k, v, qi, ki, wi).reshape(nb, t, ATTN_W)
    x = x + gate1 * (jnp.concatenate([a_out, b_out], axis=-1) @ w_out)
    h2 = rms_norm(x, norm2_g) * (1 + scale2) + shift2
    x = x + gate2 * (jnp.square(jax.nn.relu(h2 @ w_ff1)) @ w_ff2)
    return x, k, v, ki, u_ext[:, -(CONV_W - 1):]

def setup_inputs(seed: int = 0) -> dict:
    key = jax.random.key(seed)
    ks = iter(jax.random.split(key, 32))

    def nrm(shape, scale):
        return jax.random.normal(next(ks), shape, F32) * scale

    n_pages = PAST_LEN // PAGE_SIZE
    n_used = DEC_BATCH * n_pages
    n_pool = n_used + n_used // 4
    x_prompt = nrm((BATCH, SEQ, D_MODEL), 1.0)
    x_sample = nrm((DEC_BATCH, DEC_SEQ, D_MODEL), 1.0)
    cache_k = nrm((DEPTH, n_pool, PAGE_SIZE, N_HEADS, HEAD_DIM), 1.0)
    cache_v = nrm((DEPTH, n_pool, PAGE_SIZE, N_HEADS, HEAD_DIM), 1.0)
    cache_kidx = nrm((DEPTH, n_pool, PAGE_SIZE, D_IDX), 1.0)
    state_conv = nrm((DEPTH, DEC_BATCH, CONV_W - 1, C_CONV), 0.5)
    page_table = jax.random.permutation(next(ks), n_pool)[:n_used].reshape(DEC_BATCH, n_pages).astype(jnp.int32)
    c_prompt = nrm((BATCH, D_MODEL), 1.0)
    c_sample = nrm((DEC_BATCH, D_MODEL), 1.0)
    return {
        'x_prompt': x_prompt,
        'x_sample': x_sample,
        'cache_k': cache_k,
        'cache_v': cache_v,
        'cache_kidx': cache_kidx,
        'state_conv': state_conv,
        'page_table': page_table,
        'c_prompt': c_prompt,
        'c_sample': c_sample,
        'norm1_g': 1.0 + nrm((DEPTH, D_MODEL), 0.02),
        'w_ada': nrm((DEPTH, D_MODEL, 6 * D_MODEL), D_MODEL ** -0.5),
        'b_ada': nrm((DEPTH, 6 * D_MODEL), 0.02),
        'w_in': nrm((DEPTH, D_MODEL, D_IN), D_MODEL ** -0.5),
        'conv_w': nrm((DEPTH, CONV_W, C_CONV), CONV_W ** -0.5),
        'conv_b': nrm((DEPTH, C_CONV), 0.02),
        'conv_ln_g': 1.0 + nrm((DEPTH, C_CONV), 0.02),
        'conv_ln_b': nrm((DEPTH, C_CONV), 0.02),
        'w_out': nrm((DEPTH, MIX_WIDTH, D_MODEL), MIX_WIDTH ** -0.5),
        'norm2_g': 1.0 + nrm((DEPTH, D_MODEL), 0.02),
        'w_ff1': nrm((DEPTH, D_MODEL, D_FF), D_MODEL ** -0.5),
        'w_ff2': nrm((DEPTH, D_FF, D_MODEL), D_FF ** -0.5),
        'final_g': 1.0 + nrm((D_MODEL,), 0.02),
    }

def reference(x_prompt, x_sample, cache_k, cache_v, cache_kidx, state_conv, page_table, c_prompt, c_sample,
              norm1_g, w_ada, b_ada, w_in, conv_w, conv_b, conv_ln_g, conv_ln_b, w_out, norm2_g,
              w_ff1, w_ff2, final_g):
    past = page_table.shape[1] * PAGE_SIZE
    pos_p = jnp.arange(x_prompt.shape[1])
    pos_s = past + jnp.arange(x_sample.shape[1])
    xp, xs = x_prompt, x_sample
    kp, vp, kip, cp, ksl, vsl, kis, cs = [], [], [], [], [], [], [], []
    for l in range(DEPTH):
        w = (norm1_g[l], w_ada[l], b_ada[l], w_in[l], conv_w[l], conv_b[l], conv_ln_g[l], conv_ln_b[l],
             w_out[l], norm2_g[l], w_ff1[l], w_ff2[l])
        conv0 = jnp.zeros((xp.shape[0], CONV_W - 1, C_CONV), xp.dtype)
        xp, k1, v1, ki1, c1 = hybrid_layer(xp, c_prompt, pos_p, conv0, sparse_attend_prompt, *w)

        def attend_s(q, k, v, qi, ki, wi, layer=l):
            return sparse_attend_sample(q, k, v, qi, ki, wi, cache_k, cache_v, cache_kidx, page_table, layer)

        xs, k2, v2, ki2, c2 = hybrid_layer(xs, c_sample, pos_s, state_conv[l], attend_s, *w)
        kp.append(k1); vp.append(v1); kip.append(ki1); cp.append(c1)
        ksl.append(k2); vsl.append(v2); kis.append(ki2); cs.append(c2)
    y_prompt = rms_norm(xp, final_g)
    y_sample = rms_norm(xs, final_g)
    k_prompt, v_prompt, kidx_prompt, conv_prompt = jnp.stack(kp), jnp.stack(vp), jnp.stack(kip), jnp.stack(cp)
    k_sample, v_sample, kidx_sample, conv_sample = jnp.stack(ksl), jnp.stack(vsl), jnp.stack(kis), jnp.stack(cs)
    return (y_prompt, y_sample, k_prompt, v_prompt, kidx_prompt, conv_prompt,
            k_sample, v_sample, kidx_sample, conv_sample)


_drawn_inputs = setup_inputs


def setup_inputs(seed=0):
    import zlib

    import numpy as np

    out = dict(_drawn_inputs(seed))
    spreads = {}
    factors = {'norm1_g': 2.83,
     'conv_b': 5.823,
     'conv_ln_g': 22.468,
     'conv_ln_b': 57.193,
     'norm2_g': 9.889,
     'final_g': 21.907}
    for name, (base, spread) in spreads.items():
        noise = np.random.default_rng([zlib.crc32(name.encode()), seed]).standard_normal(out[name].shape)
        drawn = base * np.exp(spread * noise) if base else spread * noise
        out[name] = __import__('jax').numpy.asarray(drawn.astype(out[name].dtype))
    for name, factor in factors.items():
        out[name] = (out[name] * factor).astype(out[name].dtype)
    return out
```

```python
import concourse.bass as bass
from concourse import mybir

F32 = mybir.dt.float32
F32R = mybir.dt.float32r
U32 = mybir.dt.uint32
I32 = mybir.dt.int32
ACT = mybir.ActivationFunctionType
ALU = mybir.AluOpType
AX = mybir.AxisListType.X
ds = bass.ds

P = 128
D = 2048
KT = D // P
NP = 512
NS = 8
N = NP + NS
NH = N // 2
QT = NP // P
C = 1024
CT = C // P
H = 8
HI = 16
DI = 64
W = 31
PAST = 1024
PAGE = 128
PAGES = PAST // PAGE
NK = PAST + 1
TOPP = 128
TOPS = 256
FF = 8192
FB = 8
BLOCKS = FF // (FB * P)
EPS = 1e-6
TAKEN = -3.0e38
FUTURE = -1.0e38
TAKEN_BELOW = -2.0e38
MASKED = -1.0e30
SCALE = 128.0 ** -0.5

UPT = 4
KU = 4
RAW = 4
SPLIT = 8
T_QI, T_MISC, T_Q, T_K, T_V, T_CONV, T_OUT, T_FF = 0, 8, 9, 17, 25, 33, 49, 65
U_FF = T_FF * UPT
U_BLOCK = FB * UPT + KT * 2
T_BLOCK = FB + KT
U_ALL = U_FF + BLOCKS * U_BLOCK
MISC_COL = 6224 - P
MISC_SKIP = P - DI - HI
ADA_FIRST = 14
ADA_OUT = KT // 2
ADA_GAP = 24 - ADA_FIRST - ADA_OUT


def build(nc, a, o):
    def at(name, shape, dt, offset):
        return nc.alloc_sbuf_tensor_at(name, shape, dt, offset=offset)

    def size(shape):
        n = 4
        for s in shape[1:]:
            n *= s
        return (n + 31) // 32 * 32

    def region(start):
        here = [start]

        def put(name, shape, dt=F32):
            t = at(name, shape, dt, here[0])
            here[0] += size(shape)
            assert here[0] <= 229344, (name, here[0])
            return t
        put.here = here
        return put

    keep = region((nc.sbuf_base + 31) // 32 * 32)
    act_at = keep.here[0]
    a_hi = keep("a_hi", [P, KT, N], F32R)
    a_lo = keep("a_lo", [P, KT, N], F32R)
    raw = keep("raw", [P, RAW, KU * P])
    w_at = keep.here[0]
    w_hi = keep("w_hi", [P, SPLIT, KU, P], F32R)
    w_lo = keep("w_lo", [P, SPLIT, KU, P], F32R)
    ident = keep("ident", [P, P])
    ones = keep("ones", [P, P])
    mod = keep("mod", [P, 96, 9])
    vec = keep("vec", [P, 56])
    bada = keep("bada", [P, 96])
    cw = keep("cw", [P, CT, W + 1])
    gain = keep("gain", [P, 2, KT, 9])
    cT = keep("cT", [P, KT, 18], F32R)
    X = keep.here[0]

    r0 = region(act_at)
    ada = r0("ada", [P, 4, 4 * 512])
    ada_hi = r0("ada_hi", [P, 2, 4 * 512], F32R)
    ada_lo = r0("ada_lo", [P, 2, 4 * 512], F32R)
    vrow = r0("vrow", [P, P])
    brow = r0("brow", [P, P])
    assert r0.here[0] <= act_at + 2 * 33280
    xtok = at("xtok", [P, 2, D], F32, X)
    s0 = region(X + 2 * 16640)
    xrow = s0("xrow", [NS, D])
    crow = s0("crow", [9, D])
    assert s0.here[0] <= X + 3 * 16640, s0.here
    prow = at("prow", [1, NS * PAGES], I32, w_at)
    kraw = at("kraw", [P, NS // 2, PAGES, 2, DI], F32, w_at + 16384)
    kisT = at("kisT", [P, NS // 2, PAST], F32, X + 16640)
    XT = X + 3 * 16640
    sx = region(XT)
    xT = sx("xT", [P, KT, N])
    stat = region(sx.here[0])
    rstd = stat("rstd", [P, N])
    sq = stat("sq", [P, 2, N])
    cwrow = at("cwrow", [W, C], F32, stat.here[0])
    t1 = stat("t1", [P, 2, N])
    hs = stat("hs", [P, KT, NS])
    arow = stat("arow", [18, 512])
    csil = at("csil", [9, D], F32, XT)

    m0 = region(X)
    q = m0("q", [P, H, N])
    k = m0("k", [P, H, N])
    conv = m0("conv", [P, CT, N])
    qi = at("qi", [P, HI // 2, N], F32, X + 2 * 16640)
    sc = m0("sc", [P, 1280])
    wtok = m0("wtok", [P, QT, HI])
    vs = m0("vs", [P, H, NS])
    rows = m0("rows", [P, 2, NS], U32)
    smask = m0("smask", [P, 2, NS])
    snew = m0("snew", [H, NS])
    m8 = m0("m8", [P, 4, 8])
    sm = at("sm", [H, TOPS + 1], F32, m0.here[0])
    sidx = m0("sidx", [NS, TOPS + 8])
    pq = m0("pq", [P, HI, NS])
    e0 = region(m0.here[0])
    iu = at("iu", [NS, 2, TOPS], U32, e0.here[0])
    rope = e0("rope", [P, 4, N])
    sw = e0("sw", [P, 2, N])
    kv = e0("kv", [P, 2, N])
    kiT = e0("kiT", [P, N])
    wiT = e0("wiT", [HI, N])
    kvst = at("kvst", [P, 2, QT * P], F32, X + 2 * 16640)
    kvsts = at("kvsts", [NS, 2, P], F32, X + 2 * 16640 + 4096)
    kio = at("kio", [P, QT * DI + DI], F32, X)
    fi = at("fi", [NS, 4, TOPS], F32, e0.here[0])
    rs = e0("rs", [P, 2, 512])
    ssc = e0("ssc", [NS, NK + 7])
    wisel = e0("wisel", [HI, NS, NS])
    qis = e0("qis", [DI, HI, NS])
    qisb = e0("qisb", [P, 2, HI])
    wib = e0("wib", [HI, NS])
    caus = e0("caus", [P, P])
    onehot = e0("onehot", [HI, NS, NS])
    ptab = e0("ptab", [NS, PAGES], I32)
    ptf = e0("ptf", [NS, PAGES])
    i8 = e0("i8", [NS, 2, 8], U32)
    wis8 = e0("wis8", [NS, HI])
    nw = e0("nw", [NS, HI * NS])
    l0 = region(m0.here[0])
    kg = l0("kg", [P, 2, C])
    vg = l0("vg", [P, 2, C])
    vh = l0("vh", [P, QT, P])
    pr = l0("pr", [P, 1280])
    qh = l0("qh", [P, N])
    qsb = l0("qsb", [P, H])
    u = l0("u", [P, W - 1 + NP])
    us = l0("us", [P, NS, W])
    ua = l0("ua", [P, N])
    sg = l0("sg", [P, N])
    ust = at("ust", [P, NS, W], F32, l0.here[0])
    acc = l0("acc", [P, 2, NP])
    st = l0("st", [120, 2, P])
    ost = l0("ost", [32 + NS, P])
    sT = l0("sT", [P, 2, H])
    pTs = l0("pTs", [P, 2, H])
    cwb = l0("cwb", [P, W + 1])
    ridx = l0("ridx", [P, 2], U32)
    pm = l0("pm", [P, 16])
    ssm = l0("ssm", [H, 4])
    yb = l0("yb", [P, NS])
    yb2 = l0("yb2", [P, NS])
    dg = l0("dg", [H, H])

    adl = at("adl", [P, 2, 4 * 512], F32, X + 16640)
    adl_hi = at("adl_hi", [P, 2, 4 * 512], F32R, X)
    adl_lo = at("adl_lo", [P, 2, 4 * 512], F32R, X + 2 * 16640)
    b_hi = at("b_hi", [P, FB, N], F32R, X)
    b_lo = at("b_lo", [P, FB, N], F32R, X + 16640)
    tl = region(act_at)
    grow = tl("grow", [P, D])
    yrow = tl("yrow", [P, 2, D])
    fsq = tl("fsq", [P, D])
    fstat = tl("fstat", [P, 5, 8])

    ps = nc.alloc_psum_tensor("ps", [P, 8, 512], F32)
    xspill = nc.dram_tensor("xspill", [P, KT * N], F32).ap()

    def sem(name):
        return nc.alloc_semaphore(name)

    raw_landed = [sem(f"raw_landed{i}") for i in range(RAW)]
    ada_landed = [sem(f"ada_landed{i}") for i in range(4)]
    adl_landed = [sem("adl_landed0"), sem("adl_landed1")]
    hi_done, lo_done, split_used = sem("hi_done"), sem("lo_done"), sem("split_used")
    acc_done = sem("acc_done")
    free_dve, free_act = sem("free_dve"), sem("free_act")

    c_in, vec_in, ident_in, const_in, pt_in, xs_in = (
        sem("c_in"), sem("vec_in"), sem("ident_in"), sem("const_in"), sem("pt_in"), sem("xs_in"))
    x_in = [sem("x_in0"), sem("x_in1")]
    ones_set, silu_sig, silu_done = sem("ones_set"), sem("silu_sig"), sem("silu_done")
    c_tr, c_ready, vec_tr, vec_ready = sem("c_tr"), sem("c_ready"), sem("vec_tr"), sem("vec_ready")
    x_tr, x_copied_dve, x_copied_act = sem("x_tr"), sem("x_copied_dve"), sem("x_copied_act")
    ada_hi_done, ada_lo_done, ada_used, ada_row, ada_tr, mod_done = (
        sem("ada_hi_done"), sem("ada_lo_done"), sem("ada_used"), sem("ada_row"), sem("ada_tr"), sem("mod_done"))
    sq_done, sq_summed, var_mm, var_done, std_done, rstd_done = (
        sem("sq_done"), sem("sq_summed"), sem("var_mm"), sem("var_done"), sem("std_done"), sem("rstd_done"))
    t1_done, nhi_done, nlo_done, gain_done = sem("t1_done"), sem("nhi_done"), sem("nlo_done"), sem("gain_done")
    hs_done, hs_hi, spilled, reloaded = sem("hs_done"), sem("hs_hi"), sem("spilled"), sem("reloaded")
    swapped, ki_dup, wi_ready = sem("swapped"), sem("ki_dup"), sem("wi_ready")
    mt_tr, mt_dve, mt_act, kidx_stored = sem("mt_tr"), sem("mt_dve"), sem("mt_act"), sem("kidx_stored")
    isc_done, isc_relu, isc_added = sem("isc_done"), sem("isc_relu"), sem("isc_added")
    qis_set, pq_done, nw_mm, nw_done, kraw_in = (
        sem("qis_set"), sem("pq_done"), sem("nw_mm"), sem("nw_done"), sem("kraw_in"))
    kid_tr, kis_act, kis_dve, qisb_set, sdots, srelu, ssum, sadd = (
        sem("kid_tr"), sem("kis_act"), sem("kis_dve"), sem("qisb_set"), sem("sdots"), sem("srelu"), sem("ssum"), sem("sadd"))
    k_copied, kv_tr, kv_staged = sem("k_copied"), sem("kv_tr"), sem("kv_staged")
    kv_stored = [sem("kv_stored0"), sem("kv_stored1")]
    idx_ready, idx_tr, rows_ready, snew_ready = sem("idx_ready"), sem("idx_tr"), sem("rows_ready"), sem("snew_ready")
    qh_set, s_mm, p_max, p_exp, p_inv, p_ready, p_tr, pT_ready, pv_mm, pv_out = (
        sem("qh_set"), sem("s_mm"), sem("p_max"), sem("p_exp"), sem("p_inv"), sem("p_ready"), sem("p_tr"),
        sem("pT_ready"), sem("pv_mm"), sem("pv_out"))
    vh_in, st_in, kg_in, vg_in, ridx_set = sem("vh_in"), sem("st_in"), sem("kg_in"), sem("vg_in"), sem("ridx_set")
    qsb_set, qb_mm, km_done, sT_tr, s_max, s_exp, s_ready, sp_tr, pTs_ready, pvs_mm, pvs_out = (
        sem("qsb_set"), sem("qb_mm"), sem("km_done"), sem("sT_tr"), sem("s_max"), sem("s_exp"), sem("s_ready"),
        sem("sp_tr"), sem("pTs_ready"), sem("pvs_mm"), sem("pvs_out"))
    u_ready, u_staged, us_stated, u_stored, state_out = (
        sem("u_ready"), sem("u_staged"), sem("us_stated"), sem("u_stored"), sem("state_out"))
    u_zero, conv_done = sem("u_zero"), sem("conv_done")
    mu_mm, csub, cnorm, csig_done, mix_done, mhi, mlo = (
        sem("mu_mm"), sem("csub"), sem("cnorm"), sem("csig_done"), sem("mix_done"), sem("mhi"), sem("mlo"))
    x_updated, hb_done, bhi, blo = sem("x_updated"), sem("hb_done"), sem("bhi"), sem("blo")
    g_in, f_tr, f_sum, f_var, f_std, f_y = (
        sem("g_in"), sem("f_tr"), sem("f_sum"), sem("f_var"), sem("f_std"), sem("f_y"))
    y_stored = [sem("y_stored0"), sem("y_stored1")]

    def loop(eng, n, body, first=1, last=0):
        for i in range(min(first, n)):
            body(i)
        if n - first - last == 1:
            body(first)
        elif n - first - last > 1:
            with eng.Fori(first, n - last) as i:
                body(i)
        for i in range(max(n - last, first), n):
            body(i)

    def pick(t, i):
        return t[:, ds(i, 1), :].rearrange("p a n -> p (a n)")

    def pick2(t, i):
        return t[:, ds(i, 1), :].rearrange("p a (h n) -> p (a h) n", h=2)

    def two(t):
        return t.rearrange("p (h n) -> p h n", h=2)

    def pair(T):
        return ps[:, 2 * (T % 2):2 * (T % 2) + 2, 0:NH]


    w_in = a["w_in"].rearrange("l (u k p) n -> p (l u) k n", k=KU, p=P)
    w_out = a["w_out"].rearrange("l (u k p) n -> p (l u) k n", k=KU, p=P)
    w_ff1 = a["w_ff1"].rearrange("l (u k p) n -> p (l u) k n", k=KU, p=P)
    w_ff2 = a["w_ff2"].rearrange("l (b u k p) n -> p (l b) u k n", u=2, k=KU, p=P)
    w_ada = a["w_ada"].rearrange("l (g k p) n -> p (l g) k n", k=4, p=P)
    kidx_pages = a["cache_kidx"].rearrange("l n s d -> (l n) s d")
    cache_k = a["cache_k"].rearrange("l n s h d -> (l n s) (h d)")
    cache_v = a["cache_v"].rearrange("l n s h d -> (l n s) (h d)")
    state = a["state_conv"].rearrange("l (g b) w c -> (l b w) g c", g=2)
    kv_out = [o["k_prompt"].rearrange("l b (t p) h d -> p (l b t) h d", p=P),
              o["v_prompt"].rearrange("l b (t p) h d -> p (l b t) h d", p=P)]
    kvs_out = [o["k_sample"].rearrange("l b s h d -> (l b s) h d"),
               o["v_sample"].rearrange("l b s h d -> (l b s) h d")]

    with nc.Block() as block:

        @block.sync
        def _(sp):
            sp.dma_start(crow[0:1, :], a["c_prompt"]).then_inc(c_in, 16)
            sp.dma_start(crow[1:9, :], a["c_sample"]).then_inc(c_in, 16)
            sp.dma_start(ident[:], a["const_ident"]).then_inc(ident_in, 16)
            at_row = 0
            for name, n in (("norm1_g", KT), ("norm2_g", KT), ("conv_b", CT), ("conv_ln_g", CT), ("conv_ln_b", CT)):
                sp.dma_start(vrow[at_row:at_row + n, :], a[name].rearrange("l (f p) -> (l f) p", p=P)).then_inc(vec_in, 16)
                at_row += n
            sp.dma_start(brow[0:96, :], a["b_ada"].rearrange("l (f p) -> (l f) p", p=P)).then_inc(vec_in, 16)
            sp.dma_start(cwrow[:, :], a["conv_w"].rearrange("l w c -> (l w) c")).then_inc(vec_in, 16)
            sp.dma_start(prow[:], a["page_table"].rearrange("(a b) p -> a (b p)", a=1)).then_inc(pt_in, 16)
            sp.dma_start(xrow[:], a["x_sample"].rearrange("b s d -> (b s) d")).then_inc(xs_in, 16)
            xp = a["x_prompt"].rearrange("b (t p) d -> p (b t) d", p=P)
            for t in range(QT):
                if t >= 2:
                    sp.wait_ge(x_tr, 4 * (t - 1))
                sp.dma_start(xtok[:, t % 2, :], xp[:, t, :]).then_inc(x_in[t % 2], 16)
            sp.dma_start(o["conv_sample"][0, :, 0:W - 2, :], a["state_conv"][0, :, 1:W - 1, :]).then_inc(state_out, 16)

            def load_ada(c):
                for g in range(4):
                    if not isinstance(c, int):
                        sp.wait_ge(ada_lo_done, 4 * (c - 1) + g + 1)
                    sp.dma_start(ada[:, g, :].rearrange("p (k n) -> p k n", k=4), w_ada[:, g, :, ds(c * 512, 512)]
                                 ).then_inc(ada_landed[g], 16)
            loop(sp, ADA_FIRST, load_ada)

            def load(G, src, waits=(0, 1, 2, 3)):
                for uu in range(4):
                    if (not isinstance(G, int) or G >= 1) and waits[uu] is not None:
                        sp.wait_ge(lo_done, 4 * (G - 1) + waits[uu] + 1)
                    sp.dma_start(raw[:, uu, :].rearrange("p (k m) -> p k m", k=KU), src(uu)).then_inc(raw_landed[uu], 16)

            def in_tile(T, col):
                load(T, lambda uu: w_in[:, uu, :, ds(col, P)])

            def ada_pair(c, e, n):
                for g in range(2):
                    if isinstance(n, int) and n == 0:
                        pass
                    elif isinstance(n, int) and n > 2 * ADA_OUT:
                        sp.wait_ge(ada_used, 4 * ADA_FIRST + 2 * (n - 1) + g + 1)
                    else:
                        sp.wait_ge(ada_lo_done, 4 * ADA_FIRST + 2 * (n - 1) + g + 1)
                    sp.dma_start(adl[:, g, :].rearrange("p (k n) -> p k n", k=4), w_ada[:, 2 * e + g, :, ds(c * 512, 512)]
                                 ).then_inc(adl_landed[g], 16)

            in_tile(0, 5120)
            in_tile(1, 5120 + P)
            sp.wait_ge(spilled, 16)
            sp.wait_ge(nlo_done, KT + 1)
            for i, name in enumerate(("const_cos", "const_sin", "const_icos", "const_isin")):
                sp.dma_start(rope[:, i, :], a[name]).then_inc(const_in, 16)
            sp.dma_start(caus[:], a["const_future"]).then_inc(const_in, 16)
            sp.dma_start(onehot[:], a["const_onehot"]).then_inc(const_in, 16)
            sp.dma_start(ptab[:], a["page_table"]).then_inc(const_in, 16)
            loop(sp, 6, lambda i: in_tile(T_QI + 2 + i, 5120 + (2 + i) * P), first=0)
            in_tile(T_MISC, MISC_COL)
            loop(sp, 24, lambda i: in_tile(T_Q + i, 2048 + i * P), first=0)
            def conv_tiles(j):
                in_tile(T_CONV + 2 * j, j * P)
                in_tile(T_CONV + 2 * j + 1, C + j * P)
            conv_tiles(0)

            def conv_loop(j):
                if isinstance(j, int) and j == 0:
                    sp.wait_ge(kv_stored[0], 32 * 8)
                    sp.wait_ge(kv_stored[1], 32 * 8)
                else:
                    sp.wait_ge(pv_mm, j)
                if isinstance(j, int) and j == 0:
                    sp.wait_ge(idx_tr, 1)
                sp.dma_start(vh[:], kv_out[1][:, :, ds(j, 1), :].rearrange("p t a d -> p t (a d)")).then_inc(vh_in, 16)
                if not isinstance(j, int) or j > 0:
                    sp.wait_ge(p_tr, j)
                sp.dma_start(st[:], state[:, :, ds(j * P, P)]).then_inc(st_in, 16)
                if isinstance(j, int) and j == CT - 1:
                    for i in range(2):
                        load(T_OUT + i, lambda uu, i=i: w_out[:, (uu + 2) % 4, :, i * P:(i + 1) * P])
                else:
                    conv_tiles(j + 1)
            loop(sp, CT, conv_loop, last=1)
            sp.wait_ge(s_mm, H)
            ada_pair(ADA_FIRST, 0, 0)

            def out_tiles(i):
                for e in range(2):
                    load(T_OUT + 2 + 2 * i + e, lambda uu: w_out[:, (uu + 2) % 4, :, ds((2 + 2 * i + e) * P, P)],
                         waits=(0, 2, None, 3))
                    ada_pair(ADA_FIRST + i + e, 1 - e, 2 * i + e + 1)
            loop(sp, KT // 2 - 1, out_tiles)

            def up_tile(b, i):
                load(T_FF + b * 16 + i, lambda uu: w_ff1[:, uu, :, ds((b * FB + i) * P, P)])

            def block_tiles(b, i0):
                with sp.Fori(i0, FB) as i:
                    up_tile(b, i)
                with sp.Fori(0, KT // 2) as i:
                    load(T_FF + b * 16 + 8 + i,
                         lambda uu: w_ff2[:, ds(b, 1), uu % 2, :, ds((2 * i + uu // 2) * P, P)].rearrange("p a k n -> p (a k) n"))
            up_tile(0, 0)
            ada_pair(ADA_FIRST + ADA_OUT - 1, 1, 2 * ADA_OUT - 1)
            up_tile(0, 1)
            for n in range(2 * ADA_GAP):
                ada_pair(ADA_FIRST + ADA_OUT + n // 2, n % 2, 2 * ADA_OUT + n)
            with sp.Fori(0, 1) as b:
                block_tiles(b, 2)
            with sp.Fori(1, BLOCKS) as b:
                block_tiles(b, 0)
            sp.wait_ge(state_out, 16)

        @block.gpsimd
        def _(pool):
            def split_lo(G, gp):
                for uu in range(4):
                    pool.wait_ge(hi_done, 4 * G + uu + 1)
                    nc.gpsimd.tensor_tensor(w_lo[:, 4 * gp + uu, :, :].rearrange("p k m -> p (k m)"), raw[:, uu, :],
                                            w_hi[:, 4 * gp + uu, :, :].rearrange("p k m -> p (k m)").bitcast(F32),
                                            ALU.subtract).then_inc(lo_done, 1)

            def split_pair(G, gp):
                split_lo(G, gp)
                split_lo(G + 1, 1 - gp)

            nc.gpsimd.memset(ones[:], 1.0).then_inc(ones_set, 1)
            pool.wait_ge(pt_in, 16)
            with pool.Fori(0, NS // 2) as m:
                for e in range(2):
                    for page in range(PAGES):
                        r = pool.value_load(prow[0:1, ds(m * (2 * PAGES) + e * PAGES + page, 1)], min_val=0,
                                            max_val=a["cache_kidx"].shape[1] - 1)
                        pool.dma_start(kraw[:, ds(m, 1), page, e, :].rearrange("p a d -> p (a d)"),
                                       kidx_pages[ds(r, 1)].rearrange("a s d -> s (a d)")).then_inc(kraw_in, 16)
            loop(pool, 17, lambda i: split_pair(2 * i, 0), first=0)
            split_lo(34, 0)

            def gathers(j):
                pool.wait_ge(rows_ready, 1)
                if not isinstance(j, int) or j > 0:
                    pool.wait_ge(km_done, j)
                    pool.wait_ge(vg_in, 32 * j)
                nc.gpsimd.tensor_copy(ridx[:], rows[:, :, ds(j, 1)].rearrange("p t a -> p (t a)")).then_inc(ridx_set, 1)
                pool.drain()
                for t in range(2):
                    nc.gpsimd.indirect_dma_start(kg[:, t, :], None, cache_k,
                                                 bass.IndirectOffsetOnAxis(ap=ridx[:, t:t + 1], axis=0)).then_inc(kg_in, 16)
                split_lo(T_CONV + 2 + 2 * j + 1, 0)
                pool.wait_ge(rows_ready, 1)
                if isinstance(j, int) and j == 0:
                    pool.wait_ge(kv_tr, 16)
                else:
                    pool.wait_ge(pvs_mm, j)
                for t in range(2):
                    nc.gpsimd.indirect_dma_start(vg[:, t, :], None, cache_v,
                                                 bass.IndirectOffsetOnAxis(ap=ridx[:, t:t + 1], axis=0)).then_inc(vg_in, 16)

            def conv_loop(j):
                split_lo(T_CONV + 2 + 2 * j, 1)
                gathers(j)
            loop(pool, CT, conv_loop)
            loop(pool, (U_ALL // 4 - 51) // 2, lambda i: split_pair(51 + 2 * i, 1), first=0)

        @block.scalar
        def _(act):
            def copy(out, in_):
                return nc.scalar.activation(out, in_, ACT.Copy)

            def split_hi(G, gp, which=range(4)):
                for uu in which:
                    act.wait_ge(raw_landed[uu], 16 * (G + 1))
                    if not isinstance(G, int) or G >= 2:
                        act.wait_ge(split_used, 4 * G + uu - 7)
                    copy(w_hi[:, 4 * gp + uu, :, :].rearrange("p k m -> p (k m)"), raw[:, uu, :]).then_inc(hi_done, 1)

            act.wait_ge(c_in, 32)
            nc.scalar.activation(csil[:], crow[:], ACT.Sigmoid).then_inc(silu_sig, 1)
            for n in range(1, 4 * QT, 2):
                act.wait_ge(x_tr, n + 1)
                t, g = n // 4, n % 4
                copy(xT[:, 4 * g:4 * g + 4, t * P:(t + 1) * P], ps[:, 4 + n % 4, :].rearrange("p (f n) -> p f n", f=4)
                     ).then_inc(x_copied_act, 1)

            def squares(x_of, n0, count, ready):
                for f in range(count):
                    ready(f)
                    if n0 + f >= 2:
                        act.wait_ge(sq_summed, n0 + f - 1)
                    nc.scalar.activation(sq[:, f % 2, :], x_of(f), ACT.Square).then_inc(sq_done, 1)

            def std(n):
                act.wait_ge(var_done, n)
                nc.scalar.activation(rstd[:], t1[:, 1, :], ACT.Sqrt).then_inc(std_done, 1)

            def hs_split(n):
                act.wait_ge(hs_done, n)
                copy(a_hi[:, :, NP:N], hs[:]).then_inc(hs_hi, 1)

            def norm_hi(n, shift):
                for f in range(KT):
                    act.wait_ge(t1_done, KT * n + f + 1)
                    nc.scalar.activation(a_hi[:, f, 0:NP], t1[:, f % 2, 0:NP], ACT.Identity,
                                         bias=mod[:, shift + f, 0:1]).then_inc(nhi_done, 1)

            def ada_high(c):
                for g in range(4):
                    act.wait_ge(ada_landed[g], 16 * (c + 1))
                    if not isinstance(c, int) or 4 * c + g >= 2:
                        act.wait_ge(ada_used, 4 * c + g - 1)
                    copy(ada_hi[:, g % 2, :], ada[:, g, :]).then_inc(ada_hi_done, 1)

            def ada_rows(c, bank):
                act.wait_ge(ada_used, 4 * (c + 1))
                if not isinstance(c, int) or c > 0:
                    act.wait_ge(ada_tr, c)
                copy(arow[:], ps[0:18, bank, :]).then_inc(ada_row, 1)

            def ada_chunks(i):
                for e in range(2):
                    c = 2 * i + e
                    ada_high(c)
                    if not isinstance(c, int) or c > 0:
                        ada_rows(c - 1, 1 - e)
            ada_chunks(0)
            act.wait_ge(x_copied_dve, 9)
            squares(lambda f: xT[:, f, :], 0, KT, lambda f: None)
            std(1)
            ada_chunks(1)
            for m in range(NS // 2):
                act.wait_ge(kid_tr, 2 * m + 2)
                copy(kisT[:, m, 512:1024], ps[:, 5, :]).then_inc(kis_act, 1)
            loop(act, ADA_FIRST // 2 - 2, lambda i: ada_chunks(2 + i), first=0)
            ada_rows(ADA_FIRST - 1, 1)
            act.wait_ge(rstd_done, 1)
            act.dma_start(xspill, xT[:].rearrange("p f n -> p (f n)")).then_inc(spilled, 16)
            split_hi(0, 0)
            split_hi(1, 1)
            act.wait_ge(ada_used, 4 * ADA_FIRST)
            hs_split(1)
            norm_hi(0, 0)

            def swap(T, tp, step):
                act.wait_ge(split_used, 4 * (T + 1))
                if not isinstance(T, int) or T >= 2:
                    act.wait_ge(free_dve, T - 1)
                for p0 in range(0, P, 2 * step):
                    copy(two(sw[p0:p0 + step, tp, :]), pair(tp)[p0 + step:p0 + 2 * step])
                    last = copy(two(sw[p0 + step:p0 + 2 * step, tp, :]), pair(tp)[p0:p0 + step])
                last.then_inc(swapped, 1)

            def qi_body(i):
                for e in range(2):
                    if isinstance(i, int) and i == 0:
                        act.wait_ge(spilled, 16)
                        act.wait_ge(nlo_done, KT + 1)
                    swap(2 * i + e, e, 32)
                    split_hi(2 * i + e + 2, e)
            loop(act, 4, qi_body)

            act.wait_ge(split_used, 4 * (T_MISC + 1))
            act.wait_ge(free_dve, T_MISC - 1)
            copy(two(wiT[:]), pair(T_MISC)[DI:DI + HI]).then_inc(wi_ready, 1)
            copy(two(sw[0:32, 0, :]), pair(T_MISC)[32:64])
            copy(two(sw[32:64, 0, :]), pair(T_MISC)[0:32]).then_inc(swapped, 1)
            split_hi(T_MISC + 2, 0)
            act.wait_ge(free_dve, T_MISC + 1)
            copy(kiT[DI:P, :], kiT[0:DI, :]).then_inc(ki_dup, 1)
            copy(qis[:].rearrange("p (m e) b -> p m e b", e=2)[:, :, 0, :], qi[0:DI, :, NP:N])
            copy(qis[:].rearrange("p (m e) b -> p m e b", e=2)[:, :, 1, :], qi[DI:P, :, NP:N]).then_inc(qis_set, 1)
            act.wait_ge(mt_tr, 1)
            copy(kio[:, 0:QT * DI], ps[:, 6, 0:QT * DI])
            copy(kio[0:NS, QT * DI:], ps[0:NS, 7, 0:DI]).then_inc(mt_act, 1)
            act.wait_ge(mt_act, 1)
            act.dma_start(o["kidx_prompt"].rearrange("l b (t p) d -> p (l b t) d", p=P),
                          kio[:, 0:QT * DI].rearrange("p (t d) -> p t d", d=DI)).then_inc(kidx_stored, 16)
            act.dma_start(o["kidx_sample"].rearrange("l b s d -> (l b s) d"), kio[0:NS, QT * DI:]).then_inc(kidx_stored, 16)
            for n in range(3 * HI):
                act.wait_ge(isc_done, n + 1)
                if n >= 2:
                    act.wait_ge(isc_added, n - 1)
                w = (n % 3 + 2) * P
                nc.scalar.activation(rs[:, n % 2, 0:w], ps[:, 4 + n % 4, 0:w], ACT.Relu, scale=DI ** -0.5).then_inc(isc_relu, 1)

            def q_body(i):
                for e in range(2):
                    b = 2 * i + e
                    T, tp = T_Q + b, (T_Q + e) % 2
                    if isinstance(i, int) and b == 0:
                        act.wait_ge(isc_added, 3 * HI)
                        act.wait_ge(nw_done, 1)
                        act.wait_ge(kidx_stored, 32)
                    else:
                        act.wait_ge(ssum, b)
                    copy(qisb[e * DI:(e + 1) * DI, e, :], qis[:, :, ds(b, 1)].rearrange("p h a -> p (h a)"))
                    copy(wib[:], wisel[:, ds(b, 1), :].rearrange("p a n -> p (a n)")).then_inc(qisb_set, 1)
                    act.wait_ge(sdots, b + 1)
                    for c in range(2):
                        last = nc.scalar.activation(rs[0:HI, c, :], ps[0:HI, 6 + c, :], ACT.Relu, scale=DI ** -0.5)
                    last.then_inc(srelu, 1)
                    swap(T, tp, 64)
                    split_hi(T + 2, tp)
            loop(act, 4, q_body)

            def kv_flush(n, slot, out, out_s, h):
                act.wait_ge(kv_tr, n + 1)
                if not isinstance(n, int) or n >= 2:
                    act.wait_ge(kv_stored[slot], 16 * (n - slot))
                copy(kvst[:, slot, :], ps[:, 4, :])
                copy(kvsts[:, slot, :], ps[0:NS, 5, 0:P]).then_inc(kv_staged, 1)
                act.wait_ge(kv_staged, n + 1)
                act.dma_start(out[:, :, ds(h, 1), :].rearrange("p t a d -> p t (a d)"),
                              kvst[:, slot, :].rearrange("p (t d) -> p t d", d=P)).then_inc(kv_stored[slot], 16)
                act.dma_start(out_s[:, ds(h, 1), :].rearrange("p a d -> p (a d)"), kvsts[:, slot, :]).then_inc(kv_stored[slot], 16)

            def k_body(i):
                for e in range(2):
                    n = 2 * i + e
                    T, tp = T_K + n, (T_K + e) % 2
                    if not (isinstance(i, int) and n == 0):
                        kv_flush(n - 1, 1 - e, kv_out[0], kvs_out[0], n - 1)
                    swap(T, tp, 64)
                    split_hi(T + 2, tp)
                    act.wait_ge(free_dve, T + 1)
                    copy(pick(k, n), kv[:, tp, :]).then_inc(k_copied, 1)
            loop(act, 4, k_body)

            def v_body(i):
                for e in range(2):
                    n = 2 * i + e
                    T, tp = T_V + n, (T_V + e) % 2
                    if isinstance(i, int) and n == 0:
                        kv_flush(7, 1, kv_out[0], kvs_out[0], 7)
                    else:
                        kv_flush(8 + n - 1, 1 - e, kv_out[1], kvs_out[1], n - 1)
                    act.wait_ge(split_used, 4 * (T + 1))
                    act.wait_ge(kv_tr, 8 + n - 1)
                    copy(two(kv[:, tp, :]), pair(tp))
                    copy(vs[:, ds(n, 1), :].rearrange("p a n -> p (a n)"),
                         pair(tp)[:, 1, NH - NS:NH]).then_inc(free_act, 1)
                    split_hi(T + 2, tp)
            loop(act, 4, v_body)

            def lagging(jj):
                act.wait_ge(pv_mm, jj + 1)
                copy(q[:, ds(jj, 1), 0:NP].rearrange("p a n -> p (a n)"), ps[:, 7, :]).then_inc(pv_out, 1)
                act.wait_ge(s_max, jj + 1)
                nc.scalar.activation(sm[:], sm[:], ACT.Exp, bias=ssm[:, 1:2], accum_out=ssm[:, 2:3]).then_inc(s_exp, 1)

            def row_p(jj):
                act.wait_ge(sp_tr, jj + 1)
                copy(pTs[:], ps[:, 6, 256:272].rearrange("p (t h) -> p t h", t=2)).then_inc(pTs_ready, 1)

            def store_u(jj):
                copy(ost[0:W - 1, :], ps[0:W - 1, 7, 384:512])
                copy(ost[32:32 + NS, :], ps[0:NS, 5, 384:512]).then_inc(u_staged, 1)
                act.wait_ge(u_staged, jj + 1)
                act.dma_start(o["conv_prompt"].rearrange("l b w c -> (l b w) c")[:, ds(jj * P, P)], ost[0:W - 1, :]
                              ).then_inc(u_stored, 16)
                act.dma_start(o["conv_sample"].rearrange("l b w c -> b (l w) c")[:, W - 2, ds(jj * P, P)], ost[32:32 + NS, :]
                              ).then_inc(u_stored, 16)

            def conv_body(j):
                first = isinstance(j, int) and j == 0
                Ta, pa = T_CONV + 2 * j, T_CONV % 2
                if first:
                    kv_flush(15, 1, kv_out[1], kvs_out[1], 7)
                    act.wait_ge(idx_tr, 1)
                    act.wait_ge(kv_stored[0], 32 * 8)
                    act.wait_ge(kv_stored[1], 32 * 8)
                else:
                    act.wait_ge(s_mm, j)
                copy(qh[:], pick(q, j)).then_inc(qh_set, 1)
                if not first:
                    lagging(j - 1)
                split_hi(Ta + 2, pa)
                act.wait_ge(split_used, 4 * (Ta + 1))
                if not first:
                    act.wait_ge(u_ready, j)
                copy(two(ua[:]), pair(pa)).then_inc(free_act, 1)
                if not first:
                    row_p(j - 1)
                act.wait_ge(p_max, j + 1)
                for t in range(QT):
                    lo, w = t * (t + 1) // 2 * P, (t + 1) * P
                    last = nc.scalar.activation(pr[:, lo:lo + w], pr[:, lo:lo + w], ACT.Exp, bias=pm[:, 4 + t:5 + t],
                                                accum_out=pm[:, 8 + t:9 + t])
                last.then_inc(p_exp, 1)
                act.wait_ge(p_inv, j + 1)
                for t in range(QT):
                    lo, w = t * (t + 1) // 2 * P, (t + 1) * P
                    last = nc.scalar.activation(pr[:, lo:lo + w], pr[:, lo:lo + w], ACT.Copy, scale=pm[:, 12 + t:13 + t])
                last.then_inc(p_ready, 1)
                split_hi(Ta + 3, 1 - pa)
                act.wait_ge(split_used, 4 * (Ta + 2))
                nc.scalar.activation(two(sg[:]), pair(1 - pa), ACT.Sigmoid).then_inc(free_act, 1)
                act.wait_ge(p_tr, j + 1)
                copy(pr[:, 0:512], ps[:, 4, :])
                copy(pr[:, 512:896], ps[:, 5, 0:384])
                copy(pr[:, 896:1280], ps[:, 7, 0:384]).then_inc(pT_ready, 1)
                if not first:
                    if not isinstance(j, int):
                        act.wait_ge(u_stored, 32 * (j - 1))
                    store_u(j - 1)
                if not first:
                    act.wait_ge(qb_mm, j)
                copy(qsb[:], q[:, :, ds(NP + j, 1)].rearrange("p h a -> p (h a)")).then_inc(qsb_set, 1)
            loop(act, CT, conv_body, first=2)
            lagging(7)
            row_p(7)
            act.wait_ge(p_tr, CT + 1)
            act.wait_ge(u_stored, 32 * 7)
            store_u(7)

            act.wait_ge(pvs_out, NS)
            for h in range(H):
                copy(a_hi[:, CT + h, :], q[:, h, :]).then_inc(mhi, 1)
            for c in range(CT):
                act.wait_ge(csub, c + 1)
                act.wait_ge(sq_summed, KT + c - 1)
                nc.scalar.activation(sq[:, c % 2, :], conv[:, c, :], ACT.Square).then_inc(sq_done, 1)
            std(2)
            for c in range(CT):
                act.wait_ge(cnorm, c + 1)
                if c >= 2:
                    act.wait_ge(mix_done, c - 1)
                nc.scalar.activation(t1[:, c % 2, :], conv[:, c, :], ACT.Sigmoid, scale=vec[:, 40 + c:41 + c],
                                     bias=vec[:, 48 + c:49 + c]).then_inc(csig_done, 1)
                if c >= 1:
                    act.wait_ge(mix_done, c)
                    copy(a_hi[:, c - 1, :], conv[:, c - 1, :]).then_inc(mhi, 1)
            act.wait_ge(mix_done, CT)
            copy(a_hi[:, CT - 1, :], conv[:, CT - 1, :]).then_inc(mhi, 1)
            act.wait_ge(u_stored, 32 * 8)
            act.wait_ge(u_ready, CT)
            act.dma_start(xT[:].rearrange("p f n -> p (f n)"), xspill).then_inc(reloaded, 16)

            def ada_beside(i, e):
                for g in range(2):
                    act.wait_ge(adl_landed[g], 16 * (2 * i + e + 1))
                    act.wait_ge(ada_used, 4 * (ADA_FIRST + i) + 2 * e + g - 1)
                    copy(adl_hi[:, g, :], adl[:, g, :]).then_inc(ada_hi_done, 1)

            def out_body(i):
                for e in range(2):
                    T, tp = T_OUT + 2 * i + e, (T_OUT + e) % 2
                    if e == 0 and not (isinstance(i, int) and i == 0):
                        ada_rows(ADA_FIRST + i - 1, 4)
                    if isinstance(i, int) and i == 0:
                        if e == 0:
                            act.wait_ge(mlo, H)
                            ada_beside(0, 0)
                            ada_beside(0, 1)
                    else:
                        ada_beside(i, e)
                    split_hi(T + 2, tp)
                    act.wait_ge(x_updated, 2 * i + e + 1)
                    act.wait_ge(sq_summed, KT + CT + 2 * i + e - 1)
                    nc.scalar.activation(sq[:, e, :], pick(xT, 2 * i + e), ACT.Square).then_inc(sq_done, 1)
            loop(act, KT // 2, out_body)
            ada_rows(ADA_FIRST + ADA_OUT - 1, 4)
            std(3)
            hs_split(2)
            norm_hi(1, 48)
            ada_rows(22, 4)
            ada_rows(23, 6)

            def block_body(b, last=False):
                def up(i):
                    for e in range(2):
                        n = 2 * i + e
                        split_hi(T_FF + b * 16 + n + 2, (T_FF + e) % 2)
                        act.wait_ge(hb_done, b * FB + n + 1)
                        copy(pick(b_hi, n), t1[:, e, :]).then_inc(bhi, 1)
                loop(act, FB // 2, up, first=0)

                def down(i):
                    for e in range(2):
                        split_hi(T_FF + b * 16 + 8 + 2 * i + e + 2, (T_FF + e) % 2)
                loop(act, FB // 2 - int(last), down, first=0)
            with act.Fori(0, BLOCKS - 1) as b:
                block_body(b)
            block_body(BLOCKS - 1, last=True)

            act.dma_start(grow[:], a["final_g"].rearrange("(a n) -> a n", a=1).broadcast_to([P, D])).then_inc(g_in, 16)
            for t in range(QT + 1):
                n = P if t < QT else NS
                act.wait_ge(f_tr, t + 1)
                if t >= 1:
                    act.wait_ge(f_y, t)
                nc.scalar.activation(fsq[0:n, :], ps[0:n, 4 * (t % 2):4 * (t % 2) + 4, :].rearrange("p a n -> p (a n)"), ACT.Square,
                                     accum_out=fstat[0:n, t, 0:1]).then_inc(f_sum, 1)
                act.wait_ge(f_var, t + 1)
                nc.scalar.activation(fstat[0:n, t, 2:3], fstat[0:n, t, 1:2], ACT.Sqrt).then_inc(f_std, 1)
                act.wait_ge(f_y, t + 1)
                act.dma_start((o["y_prompt"].rearrange("b (t p) d -> p (b t) d", p=P)[:, t, :] if t < QT
                               else o["y_sample"].rearrange("b s d -> (b s) d")), yrow[0:n, t % 2, :]).then_inc(y_stored[t % 2], 16)
            act.wait_ge(y_stored[0], 48)
            act.wait_ge(y_stored[1], 32)
            act.wait_ge(spilled, 16)

        @block.vector
        def _(dve):
            V = nc.vector
            dve.wait_ge(c_in, 32)
            dve.wait_ge(silu_sig, 1)
            V.tensor_tensor(csil[:], csil[:], crow[:], ALU.mult).then_inc(silu_done, 1)
            dve.wait_ge(c_tr, 1)
            c_ps = ps[:, 0, 0:KT * 9].rearrange("p (k n) -> p k n", n=9)
            V.tensor_copy(cT[:, :, 0:9], c_ps)
            dve.drain()
            V.tensor_tensor(cT[:, :, 9:18], c_ps, cT[:, :, 0:9].bitcast(F32), ALU.subtract).then_inc(c_ready, 1)
            dve.wait_ge(vec_tr, 1)
            V.tensor_copy(vec[:], ps[:, 1, 0:56])
            V.tensor_copy(bada[:], ps[:, 2, 0:96])
            V.tensor_copy(cw[:, :, 0:W], ps[:, 3, 0:CT * W].rearrange("p (c w) -> p c w", c=CT))
            dve.drain()
            V.tensor_copy(cw[:, :, W], vec[:, 32:40]).then_inc(vec_ready, 1)
            for n in range(0, 4 * QT, 2):
                dve.wait_ge(x_tr, n + 1)
                t, g = n // 4, n % 4
                V.tensor_copy(xT[:, 4 * g:4 * g + 4, t * P:(t + 1) * P], ps[:, 4 + n % 4, :].rearrange("p (f n) -> p f n", f=4)
                              ).then_inc(x_copied_dve, 1)
            dve.wait_ge(x_tr, 4 * QT + 1)
            V.tensor_copy(xT[:, :, NP:N], ps[:, 4, 0:KT * NS].rearrange("p (f n) -> p f n", f=KT)).then_inc(x_copied_dve, 1)

            def inv_std(n, width):
                dve.wait_ge(sq_summed, (KT, KT + CT, 2 * KT + CT)[n - 1])
                V.tensor_scalar(two(t1[:, 1, :]), ps[:, 6:8, 0:NH], 1.0 / width, EPS, ALU.mult, ALU.add).then_inc(var_done, 1)
                dve.wait_ge(std_done, n)
                V.reciprocal(rstd[:], rstd[:])
                dve.drain()
                V.scalar_tensor_tensor(sq[:, 0, :], rstd[:], -0.5, rstd[:], ALU.mult, ALU.mult)
                dve.drain()
                V.tensor_tensor(sq[:, 0, :], sq[:, 0, :], t1[:, 1, :], ALU.mult)
                dve.drain()
                V.scalar_tensor_tensor(rstd[:], sq[:, 0, :], 1.5, rstd[:], ALU.add, ALU.mult).then_inc(rstd_done, 1)
                dve.drain()

            def ada_low(c):
                for g in range(4):
                    dve.wait_ge(ada_hi_done, 4 * c + g + 1)
                    V.tensor_tensor(ada_lo[:, g % 2, :], ada[:, g, :], ada_hi[:, g % 2, :].bitcast(F32), ALU.subtract
                                    ).then_inc(ada_lo_done, 1)

            def mods(c, bank):
                dve.wait_ge(ada_tr, c + 1)
                parts = ps[:, bank, 0:72].rearrange("p (f n) -> p f n", f=4)
                V.tensor_copy(mod[:, ds(4 * c, 4), :], parts[:, :, 0:9])
                dve.drain()
                V.tensor_tensor(mod[:, ds(4 * c, 4), :], mod[:, ds(4 * c, 4), :], parts[:, :, 9:18], ALU.add).then_inc(mod_done, 1)

            def ada_chunks(i):
                for e in range(2):
                    ada_low(2 * i + e)
                    if not isinstance(i, int) or i > 0:
                        mods(2 * i + e - 2, 2 + e)

            def add_bias(f0, f1):
                V.tensor_tensor(mod[:, f0:f1, :], mod[:, f0:f1, :], bada[:, f0:f1].unsqueeze(2).broadcast_to([P, f1 - f0, 9]), ALU.add)
                dve.drain()

            def gains(n):
                V.scalar_tensor_tensor(gain[:, n, :, :], mod[:, 16 + 48 * n:32 + 48 * n, :], 1.0,
                                       vec[:, 16 * n:16 * n + 16].unsqueeze(2).broadcast_to([P, KT, 9]), ALU.add, ALU.mult)
                dve.drain()
            ada_chunks(0)
            inv_std(1, D)
            ada_chunks(1)
            for m in range(NS // 2):
                dve.wait_ge(kid_tr, 2 * m + 1)
                V.tensor_copy(kisT[:, m, 0:512], ps[:, 4, :]).then_inc(kis_dve, 1)
            loop(dve, ADA_FIRST // 2 - 2, lambda i: ada_chunks(2 + i), first=0)
            mods(ADA_FIRST - 2, 2)
            mods(ADA_FIRST - 1, 3)
            dve.drain()
            add_bias(0, 4 * ADA_FIRST)
            gains(0)

            def normed(n, shift):
                V.tensor_tensor(hs[:], xT[:, :, NP:N], rstd[:, NP:N].unsqueeze(1).broadcast_to([P, KT, NS]), ALU.mult)
                dve.drain()
                V.tensor_tensor(hs[:], hs[:], gain[:, n, :, 1:9], ALU.mult)
                dve.drain()
                V.tensor_tensor(hs[:], hs[:], mod[:, shift:shift + KT, 1:9], ALU.add).then_inc(hs_done, 1)

                dve.drain()

                def scaled(f):
                    if f >= 2:
                        dve.wait_ge(nlo_done, (KT + 1) * n + f)
                    if n or f >= 2:
                        dve.wait_ge(nhi_done, KT * n + max(f - 1, 0))
                    V.scalar_tensor_tensor(t1[:, f % 2, 0:NP], xT[:, f, 0:NP], gain[:, n, f, 0:1], rstd[:, 0:NP],
                                           ALU.mult, ALU.mult).then_inc(t1_done, 1)

                def low(f):
                    dve.wait_ge(nhi_done, KT * n + f + 1)
                    V.scalar_tensor_tensor(a_lo[:, f, 0:NP], t1[:, f % 2, 0:NP], mod[:, shift + f, 0:1],
                                           a_hi[:, f, 0:NP].bitcast(F32), ALU.add, ALU.subtract).then_inc(nlo_done, 1)
                scaled(0)
                dve.wait_ge(hs_hi, n + 1)
                V.tensor_tensor(a_lo[:, :, NP:N], hs[:], a_hi[:, :, NP:N].bitcast(F32), ALU.subtract).then_inc(nlo_done, 1)
                for f in range(KT):
                    if f + 1 < KT:
                        scaled(f + 1)
                    low(f)
            dve.wait_ge(ada_used, 4 * ADA_FIRST)
            normed(0, 0)

            def rotate(T, tp, cos, out):
                dve.wait_ge(swapped, T + 1)
                V.tensor_tensor(two(kv[:, tp, :]), pair(tp), two(rope[:, cos, :]), ALU.mult)
                V.tensor_tensor(sw[:, tp, :], sw[:, tp, :], rope[:, cos + 1, :], ALU.mult)
                dve.drain()
                V.tensor_tensor(out, kv[:, tp, :], sw[:, tp, :], ALU.add).then_inc(free_dve, 1)

            dve.wait_ge(const_in, 112)
            loop(dve, 4, lambda i: [rotate(2 * i + e, e, 2, pick(qi, 2 * i + e)) for e in range(2)])
            dve.wait_ge(swapped, T_MISC + 1)
            V.tensor_tensor(two(kv[0:DI, 0, :]), pair(T_MISC)[0:DI], two(rope[0:DI, 2, :]), ALU.mult)
            V.tensor_tensor(sw[0:DI, 0, :], sw[0:DI, 0, :], rope[0:DI, 3, :], ALU.mult)
            dve.drain()
            V.tensor_tensor(kiT[0:DI, :], kv[0:DI, 0, :], sw[0:DI, 0, :], ALU.add).then_inc(free_dve, 1)
            dve.wait_ge(qis_set, 1)
            V.tensor_tensor(pq[0:DI, :, :], qis[:], kiT[0:DI, NP:N].unsqueeze(1).broadcast_to([DI, HI, NS]), ALU.mult
                            ).then_inc(pq_done, 1)
            V.memset(qisb[DI:P, 0, :], 0.0)
            V.memset(qisb[0:DI, 1, :], 0.0)
            dve.wait_ge(wi_ready, 1)
            V.tensor_tensor(wisel[:], onehot[:], wiT[:, NP:N].unsqueeze(1).broadcast_to([HI, NS, NS]), ALU.mult)
            dve.drain()
            V.tensor_scalar(wisel[:], wisel[:], HI ** -0.5, None, ALU.mult)
            dve.wait_ge(mt_tr, 1)
            V.tensor_scalar(wtok[:], ps[:, 4, 0:QT * HI].rearrange("p (t h) -> p t h", t=QT), HI ** -0.5, None, ALU.mult)
            V.tensor_scalar(wis8[:], ps[0:NS, 5, 0:HI], HI ** -0.5, None, ALU.mult).then_inc(mt_dve, 1)
            dve.wait_ge(nw_mm, 1)
            V.tensor_scalar(nw[:], ps[0:NS, 5, 0:HI * NS], DI ** -0.5, 0.0, ALU.mult, ALU.max).then_inc(nw_done, 1)
            dve.drain()
            nw3 = nw[:].rearrange("p (h b) -> p h b", h=HI)
            V.tensor_tensor(nw3, nw3, wis8[:].unsqueeze(2).broadcast_to([NS, HI, NS]), ALU.mult)
            dve.drain()
            V.tensor_tensor(nw3, nw3, ident[0:NS, 0:NS].unsqueeze(1).broadcast_to([NS, HI, NS]), ALU.mult)
            dve.drain()
            V.tensor_reduce(ssc[:, PAST:NK], nw[:], AX, ALU.add)
            off = [0, P, 3 * P, 6 * P]
            for n in range(3 * HI):
                t, h = n % 3 + 1, n // 3
                w = (t + 1) * P
                dve.wait_ge(isc_relu, n + 1)
                s_t = sc[:, off[t]:off[t] + w]
                if h == 0:
                    V.tensor_scalar(s_t, rs[:, n % 2, 0:w], wtok[:, t, h:h + 1], None, ALU.mult).then_inc(isc_added, 1)
                else:
                    V.scalar_tensor_tensor(s_t, rs[:, n % 2, 0:w], wtok[:, t, h:h + 1], s_t, ALU.mult, ALU.add
                                           ).then_inc(isc_added, 1)
                if t == 3:
                    dve.drain()
            for t in range(1, QT):
                diag = sc[:, off[t] + t * P:off[t] + (t + 1) * P]
                V.tensor_tensor(diag, diag, caus[:], ALU.add)
            V.tensor_scalar(sc[:, 0:P], caus[:], MASKED / FUTURE, None, ALU.mult)
            dve.drain()

            def top_prompt():
                for t in range(1, QT):
                    V.max(m8[:, t, :], sc[:, off[t]:off[t] + (t + 1) * P])
                dve.drain()
                for t in range(1, QT):
                    s_t = sc[:, off[t]:off[t] + (t + 1) * P]
                    V.match_replace(s_t, m8[:, t, :], s_t, TAKEN)
                dve.drain()

            def q_body(i):
                for e in range(2):
                    b = 2 * i + e
                    T, tp = T_Q + b, (T_Q + e) % 2
                    rotate(T, tp, 0, pick(q, b))
                    dve.wait_ge(ssum, b + 1)
                    if isinstance(i, int) and b == 0:
                        V.tensor_copy(ssc[:, 0:512], ps[0:NS, 6, :])
                        V.tensor_copy(ssc[:, 512:1024], ps[0:NS, 7, :]).then_inc(sadd, 1)
                    else:
                        V.tensor_tensor(ssc[:, 0:512], ssc[:, 0:512], ps[0:NS, 6, :], ALU.add)
                        V.tensor_tensor(ssc[:, 512:1024], ssc[:, 512:1024], ps[0:NS, 7, :], ALU.add).then_inc(sadd, 1)
                    dve.drain()
                    top_prompt()
                    top_prompt()
            loop(dve, 4, q_body)
            V.tensor_scalar(sc[:, P:], sc[:, P:], TAKEN_BELOW, MASKED, ALU.is_gt, ALU.mult)

            def top_rows(r):
                V.max(m8[0:NS, 0, :], ssc[:, 0:NK])
                dve.drain()
                V.max_index(i8[:, 0, :], m8[0:NS, 0, :], ssc[:, 0:NK])
                dve.drain()
                V.match_replace(ssc[:, 0:NK], m8[0:NS, 0, :], ssc[:, 0:NK], TAKEN)
                V.tensor_copy(sidx[:, ds(r * 8, 8)], i8[:, 0, :])
                dve.drain()

            def k_body(i):
                for e in range(2):
                    n = 2 * i + e
                    T, tp = T_K + n, (T_K + e) % 2
                    if not isinstance(i, int):
                        dve.wait_ge(kv_tr, n - 1)
                        dve.wait_ge(k_copied, n - 1)
                    rotate(T, tp, 0, kv[:, tp, :])
                    top_rows(2 * n)
                    top_rows(2 * n + 1)
            loop(dve, 4, k_body)
            loop(dve, 16, lambda r: top_rows(16 + r), first=0)

            V.tensor_copy(ptf[:], ptab[:])
            V.tensor_copy(iu[:, 0, :], sidx[:, 0:TOPS])
            dve.drain()
            V.tensor_scalar(iu[:, 1, :], iu[:, 0, :], 7, None, ALU.logical_shift_right)
            dve.drain()
            V.tensor_copy(fi[:, 0, :], iu[:, 1, :])
            dve.drain()
            V.scalar_tensor_tensor(fi[:, 1, :], fi[:, 0, :], -float(PAGE), sidx[:, 0:TOPS], ALU.mult, ALU.add)
            V.tensor_scalar(fi[:, 2, :], sidx[:, 0:TOPS], float(PAST), None, ALU.is_ge)
            for page in range(PAGES):
                V.tensor_scalar(fi[:, 3, :], fi[:, 0, :], float(page), ptf[:, page:page + 1], ALU.is_equal, ALU.mult)
                dve.drain()
                V.scalar_tensor_tensor(fi[:, 1, :], fi[:, 3, :], float(PAGE), fi[:, 1, :], ALU.mult, ALU.add)
                dve.drain()
            V.reduce_max(ssc[:, 0:1], fi[:, 2, :], AX)
            dve.wait_ge(k_copied, H)
            V.tensor_tensor(pq[:, 0:H, :], q[:, :, NP:N], k[:, :, NP:N], ALU.mult).then_inc(idx_ready, 1)
            dve.wait_ge(idx_tr, 1)
            V.tensor_copy(rows[:], ps[:, 6, 0:16].rearrange("p (t b) -> p t b", t=2)).then_inc(rows_ready, 1)
            V.tensor_scalar(smask[:], ps[:, 6, 16:32].rearrange("p (t b) -> p t b", t=2), MASKED, None, ALU.mult)
            V.tensor_scalar(snew[:], ps[0:H, 6, 40:48], -MASKED, MASKED, ALU.mult, ALU.add)
            dve.drain()
            V.scalar_tensor_tensor(snew[:], ps[0:H, 6, 32:40], SCALE, snew[:], ALU.mult, ALU.add).then_inc(snew_ready, 1)

            dve.wait_ge(kv_stored[0], 32 * 8)
            dve.wait_ge(kv_stored[1], 32 * 8)
            V.memset(u[:, 0:W - 1], 0.0).then_inc(u_zero, 1)
            dve.drain()

            def taps(k0, k1):
                for w in range(k0, k1):
                    if w < 2:
                        V.tensor_scalar(acc[:, w, :], u[:, w:w + NP], cwb[:, w:w + 1], None, ALU.mult)
                    else:
                        V.scalar_tensor_tensor(acc[:, w % 2, :], u[:, w:w + NP], cwb[:, w:w + 1], acc[:, w % 2, :],
                                               ALU.mult, ALU.add)
                    if w % 2:
                        dve.drain()

            def lag_scores(jj):
                dve.wait_ge(qb_mm, jj + 1)
                dve.wait_ge(kg_in, 32 * (jj + 1))
                for t in range(2):
                    V.tensor_tensor(kg[:, t, :], kg[:, t, :], ps[:, 4:6, :].rearrange("p a n -> p (a n)"), ALU.mult)
                V.tensor_copy(cwb[:], pick(cw, jj))
                dve.drain()
                V.tensor_reduce(sT[:], kg[:].rearrange("p t (h d) -> p t h d", h=H), AX, ALU.add)
                dve.drain()
                for t in range(2):
                    last = V.tensor_scalar(sT[:, t, :], sT[:, t, :], SCALE, smask[:, t, ds(jj, 1)], ALU.mult, ALU.add)
                last.then_inc(km_done, 1)
                taps(0, 10)

            def lag_softmax(jj):
                dve.wait_ge(sT_tr, jj + 1)
                V.tensor_copy(sm[:, 0:TOPS], ps[0:H, 6, 0:TOPS])
                V.tensor_copy(sm[:, TOPS:TOPS + 1], snew[:, ds(jj, 1)])
                dve.drain()
                V.reduce_max(ssm[:, 0:1], sm[:], AX)
                dve.drain()
                V.tensor_scalar(ssm[:, 1:2], ssm[:, 0:1], -1.0, None, ALU.mult).then_inc(s_max, 1)
                taps(10, 20)
                dve.wait_ge(s_exp, jj + 1)
                V.reciprocal(ssm[:, 3:4], ssm[:, 2:3])
                dve.drain()
                V.tensor_scalar(sm[:], sm[:], ssm[:, 3:4], None, ALU.mult)
                dve.drain()
                V.tensor_scalar(dg[:], ident[0:H, 0:H], sm[:, TOPS:TOPS + 1], None, ALU.mult).then_inc(s_ready, 1)

            def lag_rest(jj):
                taps(26, W)
                dve.drain()
                V.scalar_tensor_tensor(conv[:, ds(jj, 1), 0:NP].rearrange("p a n -> p (a n)"), acc[:, 0, :], cwb[:, W:W + 1],
                                       acc[:, 1, :], ALU.add, ALU.add)
                dve.drain()
                V.tensor_tensor(ust[:], us[:], cwb[:, 0:W].unsqueeze(1).broadcast_to([P, NS, W]), ALU.mult)
                dve.drain()
                V.tensor_reduce(yb[:], ust[:], AX, ALU.add)
                dve.drain()
                V.tensor_scalar(conv[:, ds(jj, 1), NP:N].rearrange("p a n -> p (a n)"), yb[:], cwb[:, W:W + 1], None, ALU.add)
                dve.wait_ge(pvs_mm, jj + 1)
                V.tensor_tensor(yb2[:], vs[:, :, ds(jj, 1)].rearrange("p h a -> p (h a)"), ps[:, 6, 304:312], ALU.mult)
                dve.drain()
                V.tensor_tensor(q[:, :, ds(NP + jj, 1)].rearrange("p h a -> p (h a)"), yb2[:], ps[:, 6, 288:296], ALU.add
                                ).then_inc(pvs_out, 1)

            def conv_body(j):
                first = isinstance(j, int) and j == 0
                if not first:
                    lag_scores(j - 1)
                    lag_softmax(j - 1)
                dve.wait_ge(s_mm, j + 1)
                if not first:
                    dve.wait_ge(pv_mm, j)
                where = [ps[:, 5, 384:512], ps[:, 7, 0:256], ps[:, 5, 0:384], ps[:, 4, :]]
                for t in range(QT):
                    lo, w = off[t], (t + 1) * P
                    V.scalar_tensor_tensor(pr[:, lo:lo + w], where[t], SCALE, sc[:, lo:lo + w], ALU.mult, ALU.add)
                dve.drain()
                for t in range(QT):
                    V.reduce_max(pm[:, t:t + 1], pr[:, off[t]:off[t] + (t + 1) * P], AX)
                dve.drain()
                V.tensor_scalar(pm[:, 4:8], pm[:, 0:4], -1.0, None, ALU.mult).then_inc(p_max, 1)
                if not first:
                    taps(20, 26)
                dve.wait_ge(p_exp, j + 1)
                V.reciprocal(pm[:, 12:16], pm[:, 8:12]).then_inc(p_inv, 1)
                if not first:
                    lag_rest(j - 1)
                dve.wait_ge(p_tr, j + 1)
                V.tensor_copy(us[:, :, 0:W - 1], ps[:, 6, 0:240].rearrange("p (b w) -> p b w", b=NS)).then_inc(us_stated, 1)
                dve.wait_ge(free_act, T_CONV - T_V + 2 * j + 2)
                V.tensor_tensor(u[:, W - 1:W - 1 + NP], ua[:, 0:NP], sg[:, 0:NP], ALU.mult)
                V.tensor_tensor(us[:, :, W - 1], ua[:, NP:N], sg[:, NP:N], ALU.mult).then_inc(u_ready, 1)
                dve.drain()
            loop(dve, CT, conv_body)
            lag_scores(7)
            lag_softmax(7)
            taps(20, 26)
            lag_rest(7)
            dve.drain()

            dve.wait_ge(p_tr, CT + 1)
            dve.wait_ge(mu_mm, 1)
            V.tensor_scalar(two(t1[:, 0, :]), ps[:, 6:8, 0:NH], 1.0 / C, None, ALU.mult)
            dve.drain()
            for c in range(CT):
                V.tensor_tensor(conv[:, c, :], conv[:, c, :], t1[:, 0, :], ALU.subtract).then_inc(csub, 1)
            for h in range(H):
                dve.wait_ge(mhi, h + 1)
                V.tensor_tensor(a_lo[:, CT + h, :], q[:, h, :], a_hi[:, CT + h, :].bitcast(F32), ALU.subtract).then_inc(mlo, 1)
            inv_std(2, C)

            def c_norm(c):
                V.tensor_tensor(conv[:, c, :], conv[:, c, :], rstd[:], ALU.mult).then_inc(cnorm, 1)

            def c_low(c):
                dve.wait_ge(mhi, H + c + 1)
                V.tensor_tensor(a_lo[:, c, :], conv[:, c, :], a_hi[:, c, :].bitcast(F32), ALU.subtract).then_inc(mlo, 1)
            c_norm(0)
            for c in range(CT):
                if c + 1 < CT:
                    c_norm(c + 1)
                dve.wait_ge(csig_done, c + 1)
                V.tensor_scalar(conv[:, c, :], conv[:, c, :], vec[:, 40 + c:41 + c], vec[:, 48 + c:49 + c], ALU.mult, ALU.add)
                dve.drain()
                V.tensor_tensor(conv[:, c, :], conv[:, c, :], t1[:, c % 2, :], ALU.mult).then_inc(mix_done, 1)
                if c >= 1:
                    c_low(c - 1)
            c_low(CT - 1)

            def residual(units, m, gate, tp):
                dve.wait_ge(split_used, units)
                acc_p = pair(tp)
                xm = pick(xT, m)
                g0 = mod[:, ds(gate + m, 1), 0:1].rearrange("p a n -> p (a n)")
                gs = mod[:, ds(gate + m, 1), 1:9].rearrange("p a n -> p (a n)")
                V.scalar_tensor_tensor(xm[:, 0:NH], acc_p[:, 0, :], g0, xm[:, 0:NH], ALU.mult, ALU.add)
                V.scalar_tensor_tensor(xm[:, NH:NP], acc_p[:, 1, 0:NP - NH], g0, xm[:, NH:NP], ALU.mult, ALU.add)
                V.tensor_tensor(hs[:, tp, :], acc_p[:, 1, NP - NH:NH], gs, ALU.mult).then_inc(free_dve, 1)
                dve.drain()
                V.tensor_tensor(xm[:, NP:N], xm[:, NP:N], hs[:, tp, :], ALU.add).then_inc(x_updated, 1)

            dve.wait_ge(reloaded, 16)
            dve.drain()
            def ada_beside(i, e):
                for g in range(2):
                    n = 4 * (ADA_FIRST + i) + 2 * e + g
                    dve.wait_ge(ada_hi_done, n + 1)
                    dve.wait_ge(ada_used, n - 1)
                    V.tensor_tensor(adl_lo[:, g, :], adl[:, g, :], adl_hi[:, g, :].bitcast(F32), ALU.subtract
                                    ).then_inc(ada_lo_done, 1)

            def out_body(i):
                for e in range(2):
                    if isinstance(i, int) and i == 0:
                        if e == 0:
                            ada_beside(0, 0)
                            ada_beside(0, 1)
                    else:
                        ada_beside(i, e)
                    residual(4 * (T_OUT + 2 * i + e + 1), 2 * i + e, 32, (T_OUT + e) % 2)
                    if e == 1 and not (isinstance(i, int) and i == 0):
                        mods(ADA_FIRST + i - 1, 5)
            loop(dve, KT // 2, out_body)
            dve.drain()
            mods(ADA_FIRST + ADA_OUT - 1, 5)
            dve.drain()
            add_bias(4 * ADA_FIRST, 4 * (ADA_FIRST + ADA_OUT))
            gains(1)
            inv_std(3, D)
            normed(1, 48)
            for c in range(24 - ADA_GAP, 24):
                mods(c, 5)
            dve.drain()
            add_bias(96 - 4 * ADA_GAP, 96)

            def up(b, i):
                for e in range(2):
                    n = 2 * i + e
                    tp = (T_FF + e) % 2
                    dve.wait_ge(split_used, U_FF + b * U_BLOCK + 4 * (n + 1))
                    V.tensor_scalar(two(sq[:, e, :]), pair(tp), 0.0, None, ALU.max)
                    dve.drain()
                    V.tensor_tensor(two(t1[:, e, :]), two(sq[:, e, :]), pair(tp), ALU.mult).then_inc(hb_done, 1)
                    dve.wait_ge(bhi, b * FB + n + 1)
                    V.tensor_tensor(pick(b_lo, n), t1[:, e, :], pick(b_hi, n).bitcast(F32), ALU.subtract).then_inc(blo, 1)

            def down(b, i):
                for e in range(2):
                    residual(U_FF + b * U_BLOCK + 4 * FB + 2 * (2 * i + e + 1), 2 * i + e, 80, (T_FF + e) % 2)
            with dve.Fori(0, BLOCKS) as b:
                with dve.Fori(0, FB // 2) as i:
                    up(b, i)
                with dve.Fori(0, KT // 2) as i:
                    down(b, i)

            dve.wait_ge(g_in, 16)
            for t in range(QT + 1):
                n = P if t < QT else NS
                dve.wait_ge(f_sum, t + 1)
                V.tensor_scalar(fstat[0:n, t, 1:2], fstat[0:n, t, 0:1], 1.0 / D, EPS, ALU.mult, ALU.add).then_inc(f_var, 1)
                dve.wait_ge(f_std, t + 1)
                V.reciprocal(fstat[0:n, t, 3:4], fstat[0:n, t, 2:3])
                dve.drain()
                V.tensor_scalar(fstat[0:n, t, 4:5], fstat[0:n, t, 3:4], fstat[0:n, t, 3:4], -0.5, ALU.mult, ALU.mult)
                dve.drain()
                V.tensor_scalar(fstat[0:n, t, 4:5], fstat[0:n, t, 4:5], fstat[0:n, t, 1:2], 1.5, ALU.mult, ALU.add)
                dve.drain()
                V.tensor_scalar(fstat[0:n, t, 3:4], fstat[0:n, t, 3:4], fstat[0:n, t, 4:5], None, ALU.mult)
                dve.drain()
                if t >= 2:
                    dve.wait_ge(y_stored[t % 2], 16 * (t // 2))
                V.scalar_tensor_tensor(yrow[0:n, t % 2, :], ps[0:n, 4 * (t % 2):4 * (t % 2) + 4, :].rearrange("p a n -> p (a n)"),
                                       fstat[0:n, t, 3:4], grow[0:n, :], ALU.mult, ALU.mult).then_inc(f_y, 1)

        @block.tensor
        def _(pe):
            mm, tr = nc.tensor.matmul, nc.tensor.transpose

            def transpose(out, in_):
                n = in_.shape[0]
                return tr(out, in_, ident[0:n, 0:n])

            def by_product(out, in_):
                n = in_.shape[0]
                return mm(out, in_, ident[0:n, 0:n], start=True, stop=True)

            pe.wait_ge(ident_in, 16)
            pe.wait_ge(silu_done, 1)
            for kt in range(KT):
                last = transpose(ps[:, 0, kt * 9:kt * 9 + 9], csil[:, kt * P:(kt + 1) * P])
            last.then_inc(c_tr, 1)
            pe.wait_ge(vec_in, 16 * 7)
            transpose(ps[:, 1, 0:56], vrow[0:56, :])
            transpose(ps[:, 2, 0:96], brow[0:96, :])
            for c in range(CT):
                last = transpose(ps[:, 3, c * W:(c + 1) * W], cwrow[:, c * P:(c + 1) * P])
            last.then_inc(vec_tr, 1)
            for n in range(4 * QT):
                t, g = n // 4, n % 4
                if g == 0:
                    pe.wait_ge(x_in[t % 2], 16 * (t // 2 + 1))
                if n >= 4:
                    if n % 2:
                        pe.wait_ge(x_copied_act, (n - 4) // 2 + 1)
                    else:
                        pe.wait_ge(x_copied_dve, (n - 4) // 2 + 1)
                for f in range(4):
                    last = transpose(ps[:, 4 + n % 4, f * P:(f + 1) * P], xtok[:, t % 2, (4 * g + f) * P:(4 * g + f + 1) * P])
                last.then_inc(x_tr, 1)
            pe.wait_ge(xs_in, 16)
            pe.wait_ge(x_copied_dve, 7)
            for f in range(KT):
                last = transpose(ps[:, 4, f * NS:(f + 1) * NS], xrow[:, f * P:(f + 1) * P])
            last.then_inc(x_tr, 1)
            pe.wait_ge(ones_set, 1)

            def sum_squares(f, count, slot, n):
                pe.wait_ge(sq_done, n + 1)
                for h in range(2):
                    last = mm(ps[:, 6 + h, 0:NH], ones[:], sq[:, slot, h * NH:(h + 1) * NH], start=(f == 0), stop=(f == count - 1))
                last.then_inc(sq_summed, 1)
                return last

            def ada_group(bank, g, kt0, hi_, lo_):
                for kk in range(4):
                    for w in (hi_, lo_):
                        last = mm(ps[0:18, bank, :], cT[:, kt0 + kk, :], w[:, g, kk * 512:(kk + 1) * 512],
                                  start=(kt0 + kk == 0 and w is hi_), stop=(kt0 + kk == KT - 1 and w is lo_))
                last.then_inc(ada_used, 1)

            def mod_tr(c, bank):
                pe.wait_ge(ada_row, c + 1)
                for f in range(4):
                    last = by_product(ps[:, bank, f * 18:f * 18 + 18], arow[:, f * P:(f + 1) * P])
                last.then_inc(ada_tr, 1)

            def ada_chunks(i):
                for e in range(2):
                    c = 2 * i + e
                    if not isinstance(i, int) or i > 0:
                        pe.wait_ge(ada_row, c - 1)
                    for g in range(4):
                        pe.wait_ge(ada_lo_done, 4 * c + g + 1)
                        ada_group(e, g % 2, 4 * g, ada_hi, ada_lo)
                    if not isinstance(i, int) or c > 2:
                        pe.wait_ge(mod_done, c - 2)
                    if not isinstance(i, int) or c > 0:
                        mod_tr(c - 1, 3 - e)

            def ada_beside(i, e):
                if e == 0:
                    pe.wait_ge(ada_row, ADA_FIRST + i)
                for g in range(2):
                    pe.wait_ge(ada_lo_done, 4 * (ADA_FIRST + i) + 2 * e + g + 1)
                    ada_group(4, g, 8 * e + 4 * g, adl_hi, adl_lo)

            def late_tr(c):
                pe.wait_ge(mod_done, c)
                mod_tr(c, 5)

            pe.wait_ge(c_ready, 1)
            pe.wait_ge(vec_ready, 1)
            ada_chunks(0)
            pe.wait_ge(x_copied_act, 8)
            pe.wait_ge(x_copied_dve, 9)
            for f in range(KT):
                sum_squares(f, KT, f % 2, f)
            ada_chunks(1)
            pe.wait_ge(kraw_in, 16 * NS * PAGES)
            for n in range(NS):
                if n >= 2:
                    pe.wait_ge((kis_dve, kis_act)[n % 2], n // 2)
                for page in range(4):
                    last = transpose(ps[:, 4 + n % 2, page * P:(page + 1) * P],
                                     kraw[:, n // 2, 4 * (n % 2) + page, :, :].rearrange("p e d -> p (e d)"))
                last.then_inc(kid_tr, 1)
            loop(pe, ADA_FIRST // 2 - 2, lambda i: ada_chunks(2 + i), first=0)
            pe.wait_ge(mod_done, ADA_FIRST - 2)
            mod_tr(ADA_FIRST - 1, 3)

            def halves(T, tp, gp, uu, kk, kt, x_hi, x_lo, start, stop, skip=0):
                whi, wlo = w_hi[:, 4 * gp + uu, kk, skip:P], w_lo[:, 4 * gp + uu, kk, skip:P]
                out = [ps[0:P - skip, 2 * tp + h, 0:NH] for h in range(2)]
                for w, x, first, end in ((whi, x_hi, start, False), (whi, x_lo, False, False), (wlo, x_hi, False, stop)):
                    for h in range(2):
                        last = mm(out[h], w, x[:, kt, h * NH:(h + 1) * NH], start=first, stop=end)
                return last

            def tile(T, tp, G, gp, free, mid=None, ada_part=None, skip=0, k0=0):
                if free is not None:
                    pe.wait_ge(*free)
                for uu in range(4):
                    if uu == 2 and mid is not None:
                        mid()
                    if uu == 3 and ada_part is not None:
                        ada_part()
                    pe.wait_ge(lo_done, 4 * G + uu + 1)
                    for kk in range(4):
                        n = 4 * uu + kk
                        last = halves(T, tp, gp, uu, kk, (n + k0) % KT, a_hi, a_lo, n == 0, n == KT - 1, skip)
                    last.then_inc(split_used, 1)

            def two_tiles(T, frees, ready, ada_part=None, k0=0):
                def product(t, n, kk):
                    return halves(T + t, (T + t) % 2, (T + t) % 2, n // 4, kk, (n + k0) % KT, a_hi, a_lo, n == 0, n == KT - 1)
                for free in frees:
                    pe.wait_ge(*free)
                for n in range(KT - KU):
                    if n % 4 == 0:
                        pe.wait_ge(lo_done, 4 * (T + 1) + n // 4 + 1)
                    ready((n + k0) % KT)
                    for t in range(2):
                        product(t, n, n % 4)
                if ada_part is not None:
                    ada_part(T)
                    ada_part(T + 1)
                pe.wait_ge(lo_done, 4 * (T + 1) + 4)
                for t in range(2):
                    for n in range(KT - KU, KT):
                        if t == 0:
                            ready((n + k0) % KT)
                        last = product(t, n, n % 4)
                    last.then_inc(split_used, 4)

            def normed_ready(n):
                def ready(kt):
                    pe.wait_ge(nlo_done, (KT + 1) * n + kt + 2)
                return ready

            def qi_body(i):
                for e in range(2):
                    T = 2 * i + e
                    tile(T, e, T, e, (free_dve, T - 1))
            two_tiles(T_QI, [(mod_done, ADA_FIRST)], normed_ready(0))
            with pe.Fori(1, 4) as i:
                qi_body(i)
            tile(T_MISC, 0, T_MISC, 0, (free_dve, T_MISC - 1), skip=MISC_SKIP)

            pe.wait_ge(wi_ready, 1)
            for t in range(QT):
                transpose(ps[:, 4, t * HI:(t + 1) * HI], wiT[:, t * P:(t + 1) * P])
            transpose(ps[0:NS, 5, 0:HI], wiT[:, NP:N])
            pe.wait_ge(free_dve, T_MISC + 1)
            for t in range(QT):
                transpose(ps[:, 6, t * DI:(t + 1) * DI], kiT[0:DI, t * P:(t + 1) * P])
            transpose(ps[0:NS, 7, 0:DI], kiT[0:DI, NP:N]).then_inc(mt_tr, 1)
            pe.wait_ge(pq_done, 1)
            pe.wait_ge(mt_dve, 1)
            mm(ps[0:NS, 5, 0:HI * NS], ones[0:DI, 0:NS], pq[0:DI, :, :].rearrange("p h b -> p (h b)"), start=True, stop=True
               ).then_inc(nw_mm, 1)
            pe.wait_ge(ki_dup, 1)
            pe.wait_ge(mt_act, 1)
            pe.wait_ge(nw_done, 1)
            for n in range(3 * HI):
                t, h = n % 3 + 1, n // 3
                if n >= 4:
                    pe.wait_ge(isc_relu, n - 3)
                rows_ = slice(h % 2 * DI, h % 2 * DI + DI)
                mm(ps[:, 4 + n % 4, 0:(t + 1) * P], qi[rows_, h // 2, t * P:(t + 1) * P], kiT[rows_, 0:(t + 1) * P],
                   start=True, stop=True).then_inc(isc_done, 1)

            def q_body(i):
                for e in range(2):
                    b = 2 * i + e
                    T, tp = T_Q + b, (T_Q + e) % 2
                    first = isinstance(i, int) and b == 0

                    def dots():
                        pe.wait_ge(ident_in, 16)
                        if first:
                            pe.wait_ge(isc_relu, 3 * HI)
                        pe.wait_ge(qisb_set, b + 1)
                        if not first:
                            pe.wait_ge(sadd, b)
                        mm(ps[0:HI, 6, 0:HI], qisb[:, e, :], ident[:, 0:HI], start=True, stop=True)
                        for c in range(2):
                            last = mm(ps[0:HI, 6 + c, :], qisb[:, e, :],
                                      kisT[:, ds(i, 1), c * 512:(c + 1) * 512].rearrange("p a n -> p (a n)"), start=True, stop=True)
                        last.then_inc(sdots, 1)
                    tile(T, tp, T, tp, (free_dve, T - 1), mid=dots)
                    pe.wait_ge(ident_in, 16)
                    pe.wait_ge(srelu, b + 1)
                    for c in range(2):
                        last = mm(ps[0:NS, 6 + c, :], wib[:], rs[0:HI, c, :], start=True, stop=True)
                    last.then_inc(ssum, 1)
            loop(pe, 4, q_body)

            def kv_transposes(n, slot_tp, ready):
                pe.wait_ge(*ready)
                if not isinstance(n, int) or n >= 1:
                    pe.wait_ge(kv_staged, n)
                for t in range(QT):
                    transpose(ps[:, 4, t * P:(t + 1) * P], kv[:, slot_tp, t * P:(t + 1) * P])
                transpose(ps[0:NS, 5, 0:P], kv[:, slot_tp, NP:N]).then_inc(kv_tr, 1)

            def k_body(i):
                for e in range(2):
                    n = 2 * i + e
                    T, tp = T_K + n, (T_K + e) % 2
                    first = isinstance(i, int) and n == 0
                    tile(T, tp, T, tp, (free_dve, T - 1),
                         mid=None if first else lambda: kv_transposes(n - 1, 1 - tp, (free_dve, T)))
            loop(pe, 4, k_body)

            def v_body(i):
                for e in range(2):
                    n = 2 * i + e
                    T, tp = T_V + n, (T_V + e) % 2
                    if isinstance(i, int):
                        free = (free_dve, T - 1)
                        ready = (free_dve, T_V) if n == 0 else (free_act, n)
                    else:
                        free, ready = (free_act, n - 1), (free_act, n)
                    tile(T, tp, T, tp, free, mid=lambda: kv_transposes(8 + n - 1, 1 - tp, ready))
            loop(pe, 4, v_body)

            p_at = [0, 512, 896, 1152]

            def broadcast_q(jj):
                pe.wait_ge(qsb_set, jj + 1)
                for h in range(H):
                    last = mm(ps[:, 4 + h // 4, h % 4 * P:(h % 4 + 1) * P], qsb[:, h:h + 1].broadcast_to([P, P]), ident[:],
                              start=True, stop=True)
                last.then_inc(qb_mm, 1)

            def weighted_v(jj):
                pe.wait_ge(vh_in, 16 * (jj + 1))
                pe.wait_ge(pT_ready, jj + 1)
                for s in range(QT):
                    last = mm(ps[:, 7, s * P:512], vh[:, s, :], pr[:, p_at[s]:p_at[s] + (QT - s) * P], start=(s == 0),
                              stop=(s == QT - 1))
                last.then_inc(pv_mm, 1)

            def row_scores(jj):
                pe.wait_ge(ident_in, 16)
                pe.wait_ge(km_done, jj + 1)
                pe.wait_ge(us_stated, jj + 1)
                if not isinstance(jj, int) or jj > 0:
                    pe.wait_ge(s_ready, jj)
                for t in range(2):
                    last = transpose(ps[0:H, 6, t * P:(t + 1) * P], sT[:, t, :])
                last.then_inc(sT_tr, 1)

            def row_weights(jj):
                pe.wait_ge(ident_in, 16)
                pe.wait_ge(s_ready, jj + 1)
                if not isinstance(jj, int) or jj > 0:
                    pe.wait_ge(pTs_ready, jj)
                for t in range(2):
                    last = transpose(ps[:, 6, 256 + t * H:256 + (t + 1) * H], sm[:, t * P:(t + 1) * P])
                last.then_inc(sp_tr, 1)

            def row_output(jj):
                pe.wait_ge(ident_in, 16)
                pe.wait_ge(pTs_ready, jj + 1)
                pe.wait_ge(vg_in, 32 * (jj + 1))
                if not isinstance(jj, int) or jj > 0:
                    pe.wait_ge(pvs_out, jj)
                for h in range(H):
                    for t in range(2):
                        mm(ps[:, 6, 288 + h:289 + h], vg[:, t, h * P:(h + 1) * P], pTs[:, t, h:h + 1], start=(t == 0), stop=(t == 1))
                mm(ps[:, 6, 304:312], ones[0:H, :], dg[:], start=True, stop=True).then_inc(pvs_mm, 1)

            def u_transposes(jj):
                pe.wait_ge(ident_in, 16)
                pe.wait_ge(u_ready, jj + 1)
                transpose(ps[0:W - 1, 7, 384:512], u[:, NP:NP + W - 1])
                return transpose(ps[0:NS, 5, 384:512], us[:, :, W - 1])

            def conv_body(j):
                first = isinstance(j, int) and j == 0
                Ta, pa = T_CONV + 2 * j, T_CONV % 2
                if not first:
                    broadcast_q(j - 1)

                def mid_a():
                    if first:
                        kv_transposes(15, 0, (free_act, 8))
                    else:
                        weighted_v(j - 1)
                        row_scores(j - 1)
                tile(Ta, pa, Ta, pa, (free_act, Ta - 1 - T_V), mid=mid_a)
                if first:
                    pe.wait_ge(idx_ready, 1)
                    pe.wait_ge(kv_staged, 16)
                    for i, what in enumerate((1, 2)):
                        for t in range(2):
                            transpose(ps[:, 6, 16 * i + 8 * t:16 * i + 8 * t + 8], fi[:, what, t * P:(t + 1) * P])
                    for b in range(NS):
                        mm(ps[0:H, 6, 32 + b:33 + b], pq[:, 0:H, b], ones[:, 0:1], start=True, stop=True)
                    mm(ps[0:H, 6, 40:48], ssc[:, 0:1].broadcast_to([NS, H]), ident[0:NS, 0:NS], start=True, stop=True
                       ).then_inc(idx_tr, 1)
                pe.wait_ge(qh_set, j + 1)
                if not first:
                    pe.wait_ge(km_done, j)
                    pe.wait_ge(pv_out, j)
                where = [ps[:, 5, 384:512], ps[:, 7, 0:256], ps[:, 5, 0:384], ps[:, 4, :]]
                for t in range(QT):
                    last = mm(where[t], qh[:, t * P:(t + 1) * P], k[:, ds(j, 1), 0:(t + 1) * P].rearrange("p a n -> p (a n)"),
                              start=True, stop=True)
                last.then_inc(s_mm, 1)
                if not first:
                    row_weights(j - 1)
                tile(Ta + 1, 1 - pa, Ta + 1, 1 - pa, (free_act, Ta - T_V), mid=None if first else lambda: row_output(j - 1))
                pe.wait_ge(ident_in, 16)
                pe.wait_ge(st_in, 16 * (j + 1))
                if first:
                    pe.wait_ge(snew_ready, 1)
                else:
                    pe.wait_ge(pvs_out, j)
                for g in range(2):
                    transpose(ps[:, 6, 120 * g:120 * (g + 1)], st[:, g, :])
                pe.wait_ge(p_ready, j + 1)
                if not first:
                    u_transposes(j - 1)
                for s in range(QT):
                    for t in range(s, QT):
                        at_ = t * (t + 1) // 2 * P + s * P
                        out = {0: (4, 0), 1: (5, 0), 2: (7, 0), 3: (7, 256)}[s]
                        last = transpose(ps[:, out[0], out[1] + (t - s) * P:out[1] + (t - s + 1) * P], pr[:, at_:at_ + P])
                last.then_inc(p_tr, 1)
            loop(pe, CT, conv_body)
            broadcast_q(7)
            weighted_v(7)
            row_scores(7)
            row_weights(7)
            row_output(7)
            pe.wait_ge(pv_out, 8)
            pe.wait_ge(km_done, 8)
            u_transposes(7).then_inc(p_tr, 1)

            pe.wait_ge(pvs_out, NS)
            pe.wait_ge(u_staged, CT)
            for c in range(CT):
                for h in range(2):
                    last = mm(ps[:, 6 + h, 0:NH], ones[:], conv[:, c, h * NH:(h + 1) * NH], start=(c == 0), stop=(c == CT - 1))
            last.then_inc(mu_mm, 1)
            for c in range(CT):
                if c == 0:
                    pe.wait_ge(csub, 1)
                sum_squares(c, CT, c % 2, KT + c)

            def mixed(kt):
                pe.wait_ge(mlo, kt - CT + 1 if kt >= CT else H + kt + 1)
            two_tiles(T_OUT, [(free_act, T_OUT - T_V)], mixed, lambda T: ada_beside(0, T - T_OUT), k0=CT)

            def sum_squares_of(m, slot):
                pe.wait_ge(sq_done, KT + CT + m + 1)
                for h in range(2):
                    last = mm(ps[:, 6 + h, 0:NH], ones[:], sq[:, slot, h * NH:(h + 1) * NH],
                              start=isinstance(m, int) and m == 0, stop=isinstance(m, int) and m == KT - 1, skip_group_check=True)
                last.then_inc(sq_summed, 1)

            def out_body(i):
                for e in range(2):
                    m = 2 * i + e
                    T, tp = T_OUT + m, (T_OUT + e) % 2

                    def last_squares():
                        sum_squares_of(m - 2, e)
                        if e == 1:
                            late_tr(ADA_FIRST + i - 1)
                    tile(T, tp, T, tp, (free_dve, T_V + m - 1), mid=last_squares,
                         ada_part=lambda: ada_beside(i, e), k0=CT)
            out_body(1)
            with pe.Fori(2, KT // 2) as i:
                out_body(i)
            sum_squares_of(KT - 2, 0)
            sum_squares_of(KT - 1, 1)
            late_tr(23 - ADA_GAP)
            for c in range(24 - ADA_GAP, 24):
                if c == 23:
                    pe.wait_ge(var_done, 3)
                for g in range(4):
                    n = 2 * ADA_OUT + 2 * (c - 24 + ADA_GAP) + g // 2
                    pe.wait_ge(adl_landed[g % 2], 16 * (n + 1))
                    for kk in range(4):
                        last = mm(ps[0:18, 4 + 2 * (c - 22), :], cT[:, 4 * g + kk, :].bitcast(F32),
                                  adl[:, g % 2, kk * 512:(kk + 1) * 512], start=(g == 0 and kk == 0), stop=(g == 3 and kk == 3))
                    last.then_inc(ada_used, 1)

            def half_tile(T, tp, G, gp, u0, free, ready=None):
                pe.wait_ge(*free)
                for uu in (u0, u0 + 1):
                    pe.wait_ge(lo_done, 4 * G + uu + 1)
                    for kk in range(4):
                        kt = 4 * (uu - u0) + kk
                        if ready is not None:
                            ready(kt)
                        last = halves(T, tp, gp, uu, kk, kt, b_hi, b_lo, kt == 0, kt == FB - 1)
                    last.then_inc(split_used, 1)

            D0 = T_V + KT

            def block_body(b):
                first = isinstance(b, int)
                if first:
                    two_tiles(T_FF, [(free_dve, D0)], normed_ready(1), lambda T: late_tr(22 + T - T_FF))
                else:
                    for n in range(2):
                        G, par = T_FF + b * 16 + n, (T_FF + n) % 2
                        tile(G, par, G, par, (free_dve, D0 + b * KT - 1 + n))
                with pe.Fori(1, FB // 2) as i:
                    for e in range(2):
                        G, par = T_FF + b * 16 + 2 * i + e, (T_FF + e) % 2
                        tile(G, par, G, par, (hb_done, b * FB + 2 * i + e - 1))

                def down(i):
                    for e in range(2):
                        G, gp = T_FF + b * 16 + FB + 2 * i + e, (T_FF + e) % 2
                        for half in range(2):
                            m = 4 * i + 2 * e + half
                            if isinstance(i, int) and m < 2:
                                free = (hb_done, b * FB + FB - 1 + m)
                            else:
                                free = (free_dve, D0 + b * KT + m - 1)
                            half_tile(None, (T_FF + half) % 2, G, gp, 2 * half, free,
                                      (lambda kt: pe.wait_ge(blo, b * FB + kt + 1)) if isinstance(i, int) and m == 0 else None)
                loop(pe, KT // 4, down)
            block_body(0)
            with pe.Fori(1, BLOCKS) as b:
                block_body(b)

            for t in range(QT + 1):
                n = P if t < QT else NS
                if t == 0:
                    pe.wait_ge(x_updated, KT * (1 + BLOCKS))
                if t >= 2:
                    pe.wait_ge(f_y, t - 1)
                for f in range(KT):
                    last = transpose(ps[0:n, 4 * (t % 2) + f // 4, f % 4 * P:(f % 4 + 1) * P], xT[:, f, t * P:t * P + n])
                last.then_inc(f_tr, 1)


_OUTS = [("y_prompt", (1, NP, D)), ("y_sample", (NS, 1, D)), ("k_prompt", (1, 1, NP, H, P)), ("v_prompt", (1, 1, NP, H, P)),
         ("kidx_prompt", (1, 1, NP, DI)), ("conv_prompt", (1, 1, W - 1, C)), ("k_sample", (1, NS, 1, H, P)),
         ("v_sample", (1, NS, 1, H, P)), ("kidx_sample", (1, NS, 1, DI)), ("conv_sample", (1, NS, W - 1, C))]


def constants():
    import numpy as np

    pos = np.concatenate([np.arange(NP), np.full(NS, PAST)]).astype(np.float32)
    out = {}
    for name, width in (("", P), ("i", DI)):
        half = width // 2
        inv = (np.float32(10000.0) ** (-np.arange(half, dtype=np.float32) / np.float32(half))).astype(np.float32)
        ang = (pos[None, :] * inv[:, None]).astype(np.float32)
        cos, sin = np.cos(ang).astype(np.float32), np.sin(ang).astype(np.float32)
        out[f"const_{name}cos"] = np.tile(np.concatenate([cos, cos]), (P // width, 1))
        out[f"const_{name}sin"] = np.tile(np.concatenate([-sin, sin]), (P // width, 1))
    out["const_ident"] = np.eye(P, dtype=np.float32)
    q_, s_ = np.arange(P)[:, None], np.arange(P)[None, :]
    out["const_future"] = np.where(s_ > q_, np.float32(FUTURE), np.float32(0.0)).astype(np.float32)
    out["const_onehot"] = np.ascontiguousarray(np.broadcast_to(np.eye(NS, dtype=np.float32), (HI, NS, NS)))
    return out


def kernel(**inputs):
    import numpy as np
    import concourse.bacc as bacc
    from concourse.bass_utils import run_bass_kernel_spmd

    nc = bacc.Bacc("TRN2", target_bir_lowering=False, num_devices=1)
    arrays, a, o = {}, {}, {}
    for name, value in list(inputs.items()) + list(constants().items()):
        value = np.ascontiguousarray(value)
        arrays[f"in_{name}"] = value
        a[name] = nc.dram_tensor(f"in_{name}", value.shape, mybir.dt.from_np(value.dtype), kind="ExternalInput").ap()
    for name, shape in _OUTS:
        o[name] = nc.dram_tensor(f"out_{name}", shape, F32, kind="ExternalOutput").ap()
    build(nc, a, o)
    r = run_bass_kernel_spmd(nc, [arrays], core_ids=[0])
    return tuple(r.results[0][f"out_{name}"] for name, _ in _OUTS)
```

```python
import concourse.bass as bass
from concourse import mybir

F32 = mybir.dt.float32
F32R = mybir.dt.float32r
U32 = mybir.dt.uint32
I32 = mybir.dt.int32
ACT = mybir.ActivationFunctionType
ALU = mybir.AluOpType
AX = mybir.AxisListType.X
ds = bass.ds

P = 128
D = 2048
KT = D // P
NP = 512
NS = 8
N = NP + NS
NH = N // 2
QT = NP // P
C = 1024
CT = C // P
H = 8
HI = 16
DI = 64
W = 31
PAST = 1024
PAGE = 128
PAGES = PAST // PAGE
NK = PAST + 1
TOPP = 128
TOPS = 256
FF = 8192
FB = 8
BLOCKS = FF // (FB * P)
EPS = 1e-6
TAKEN = -3.0e38
FUTURE = -1.0e38
TAKEN_BELOW = -2.0e38
MASKED = -1.0e30
SCALE = 128.0 ** -0.5

UPT = 4
KU = 4
RAW = 4
SPLIT = 8
T_MISC, T_QI, T_Q, T_K, T_V, T_CONV, T_OUT, T_FF = 0, 1, 9, 17, 25, 33, 49, 65
U_FF = T_FF * UPT
U_BLOCK = FB * UPT + KT * 2
T_BLOCK = FB + KT
U_ALL = U_FF + BLOCKS * U_BLOCK
MISC_COL = 6224 - P
MISC_SKIP = P - DI - HI
ADA_FIRST = 15
ADA_OUT = KT // 2 - 1
ADA_GAP = 24 - ADA_FIRST - ADA_OUT


def build(nc, a, o):
    def at(name, shape, dt, offset):
        return nc.alloc_sbuf_tensor_at(name, shape, dt, offset=offset)

    def size(shape):
        n = 4
        for s in shape[1:]:
            n *= s
        return (n + 31) // 32 * 32

    def region(start):
        here = [start]

        def put(name, shape, dt=F32):
            t = at(name, shape, dt, here[0])
            here[0] += size(shape)
            assert here[0] <= 229344, (name, here[0])
            return t
        put.here = here
        return put

    keep = region((nc.sbuf_base + 31) // 32 * 32)
    act_at = keep.here[0]
    a_hi = keep("a_hi", [P, KT, N], F32R)
    a_lo = keep("a_lo", [P, KT, N], F32R)
    raw = keep("raw", [P, RAW, KU * P])
    w_at = keep.here[0]
    w_hi = keep("w_hi", [P, SPLIT, KU, P], F32R)
    w_lo = keep("w_lo", [P, SPLIT, KU, P], F32R)
    ident = keep("ident", [P, P])
    ones = keep("ones", [P, P])
    mod = keep("mod", [P, 96, 9])
    vec = keep("vec", [P, 56])
    bada = keep("bada", [P, 96])
    cw = keep("cw", [P, CT, W + 1])
    gain = keep("gain", [P, 2, KT, 9])
    cT = keep("cT", [P, KT, 18], F32R)
    X = keep.here[0]

    r0 = region(act_at)
    ada = r0("ada", [P, 4, 4 * 512])
    ada_hi = r0("ada_hi", [P, 4, 4 * 512], F32R)
    ada_lo = at("ada_lo", [P, 2, 4 * 512], F32R, X)
    vrow = r0("vrow", [P, P])
    brow = r0("brow", [P, P])
    assert r0.here[0] <= act_at + 2 * 33280
    xtok = at("xtok", [P, 2, D], F32, X)
    s0 = region(X + 2 * 16640)
    xrow = s0("xrow", [NS, D])
    crow = s0("crow", [9, D])
    assert s0.here[0] <= X + 3 * 16640, s0.here
    kpair = at("kpair", [P, NS // 2, 2, 4, 2, DI], F32, w_at)
    kraw = at("kraw", [P, NS // 2, 2, 2, 4 * DI], F32, w_at + 16384)
    kisT = at("kisT", [P, NS // 2, PAST], F32, X + 16640)
    XT = X + 3 * 16640
    sx = region(XT)
    xT = sx("xT", [P, KT, N])
    stat = region(sx.here[0])
    rstd = stat("rstd", [P, N])
    sq = stat("sq", [P, 2, N])
    cwrow = at("cwrow", [W, C], F32, stat.here[0])
    t1 = stat("t1", [P, 2, N])
    prow = at("prow", [1, NS * PAGES], I32, stat.here[0])
    hs = stat("hs", [P, KT, NS])
    arow = stat("arow", [18, 512])
    csil = at("csil", [9, D], F32, XT)

    m0 = region(X)
    q = m0("q", [P, H, N])
    k = m0("k", [P, H, N])
    conv = m0("conv", [P, CT, N])
    qiw = [at("qiw0", [P, HI // 2, NP - P], F32R, X), at("qiw1", [P, HI // 2, NP - P], F32R, X + 2 * 16640)]
    qid = at("qid", [P, HI // 2, NS], F32, X + 12288)
    sc = m0("sc", [P, 1280])
    wtok = m0("wtok", [P, QT, HI])
    vs = m0("vs", [P, H, NS])
    rows = m0("rows", [P, 2, NS], U32)
    smask = m0("smask", [P, 2, NS])
    snew = m0("snew", [H, NS])
    m8 = m0("m8", [P, 4, 8])
    sm = at("sm", [H, TOPS + 1], F32, m0.here[0])
    sidx = m0("sidx", [NS, TOPS + 8])
    pq = m0("pq", [P, HI, NS])
    e0 = region(m0.here[0])
    iu = at("iu", [NS, 2, TOPS], U32, e0.here[0])
    rope = e0("rope", [P, 4, N])
    sw = e0("sw", [P, 2, N])
    kv = e0("kv", [P, 2, N])
    kiT = e0("kiT", [DI, N])
    ki_hi = e0("ki_hi", [P, NP], F32R)
    ki_lo = e0("ki_lo", [P, NP], F32R)
    wiT = e0("wiT", [HI, N])
    kvst = at("kvst", [P, 2, QT * P], F32, X + 2 * 16640)
    kvsts = at("kvsts", [NS, 2, P], F32, X + 2 * 16640 + 4096)
    kio = e0("kio", [P, QT * DI + DI])
    fi = at("fi", [NS, 4, TOPS], F32, e0.here[0])
    rs = e0("rs", [P, 2, 512])
    rsd = at("rsd", [HI, 2, 512], F32, X + 2 * 16640 + 12288)
    ssc = e0("ssc", [NS, NK + 7])
    wisel = e0("wisel", [HI, NS, NS])
    qis = e0("qis", [DI, HI, NS])
    qisb = e0("qisb", [P, 2, HI])
    wib = e0("wib", [HI, NS])
    caus = e0("caus", [P, P])
    onehot = e0("onehot", [HI, NS, NS])
    ptab = e0("ptab", [NS, PAGES], I32)
    ptf = e0("ptf", [NS, PAGES])
    i8 = e0("i8", [NS, 2, 8], U32)
    wis8 = e0("wis8", [NS, HI])
    nw = e0("nw", [NS, HI * NS])
    l0 = region(m0.here[0])
    kg = l0("kg", [P, 2, C])
    vg = l0("vg", [P, 2, C])
    vh = l0("vh", [P, QT, P])
    pr = l0("pr", [P, 1280])
    qh = l0("qh", [P, N])
    qsb = l0("qsb", [P, H])
    u = l0("u", [P, W - 1 + NP])
    us = l0("us", [P, NS, W])
    ua = l0("ua", [P, N])
    sg = l0("sg", [P, N])
    ust = at("ust", [P, NS, W], F32, l0.here[0])
    acc = l0("acc", [P, 2, NP])
    st = l0("st", [120, 2, P])
    ost = l0("ost", [32 + NS, P])
    sT = l0("sT", [P, 2, H])
    pTs = l0("pTs", [P, 2, H])
    cwb = l0("cwb", [P, W + 1])
    ridx = l0("ridx", [P, 2], U32)
    pm = l0("pm", [P, 16])
    ssm = l0("ssm", [H, 4])
    yb = l0("yb", [P, NS])
    yb2 = l0("yb2", [P, NS])
    dg = l0("dg", [H, H])

    adl = at("adl", [P, 2, 4 * 512], F32, X + 16640)
    adl_hi = at("adl_hi", [P, 2, 4 * 512], F32R, X)
    adl_lo = at("adl_lo", [P, 2, 4 * 512], F32R, X + 2 * 16640)
    b_hi = at("b_hi", [P, FB, N], F32R, X)
    b_lo = at("b_lo", [P, FB, N], F32R, X + 16640)
    tl = region(act_at)
    grow = tl("grow", [P, D])
    yrow = tl("yrow", [P, 2, D])
    fsq = tl("fsq", [P, D])
    fstat = tl("fstat", [P, 5, 8])

    ps = nc.alloc_psum_tensor("ps", [P, 8, 512], F32)
    xspill = nc.dram_tensor("xspill", [P, KT * N], F32).ap()

    def sem(name):
        return nc.alloc_semaphore(name)

    raw_landed = [sem(f"raw_landed{i}") for i in range(RAW)]
    ada_landed = [sem(f"ada_landed{i}") for i in range(4)]
    adl_landed = [sem("adl_landed0"), sem("adl_landed1")]
    hi_done, lo_done, split_used = sem("hi_done"), sem("lo_done"), sem("split_used")
    acc_done = sem("acc_done")
    free_dve, free_act = sem("free_dve"), sem("free_act")

    c_in, vec_in, ident_in, const_in, pt_in, xs_in = (
        sem("c_in"), sem("vec_in"), sem("ident_in"), sem("const_in"), sem("pt_in"), sem("xs_in"))
    x_in = [sem("x_in0"), sem("x_in1")]
    ones_set, silu_sig, silu_done = sem("ones_set"), sem("silu_sig"), sem("silu_done")
    c_tr, c_ready, vec_tr, vec_ready = sem("c_tr"), sem("c_ready"), sem("vec_tr"), sem("vec_ready")
    x_tr, x_copied_dve, x_copied_act = sem("x_tr"), sem("x_copied_dve"), sem("x_copied_act")
    ada_hi_done, ada_lo_done, ada_used, ada_row, ada_tr, mod_done = (
        sem("ada_hi_done"), sem("ada_lo_done"), sem("ada_used"), sem("ada_row"), sem("ada_tr"), sem("mod_done"))
    sq_done, sq_summed, var_mm, var_done, std_done, rstd_done = (
        sem("sq_done"), sem("sq_summed"), sem("var_mm"), sem("var_done"), sem("std_done"), sem("rstd_done"))
    t1_done, nhi_done, nlo_done = sem("t1_done"), sem("nhi_done"), sem("nlo_done")
    hs_done, hs_hi, spilled, reloaded = sem("hs_done"), sem("hs_hi"), sem("spilled"), sem("reloaded")
    swapped, wi_ready, qi_hi_done, qi_lo_done, ki_hi_done, ki_lo_done = (
        sem("swapped"), sem("wi_ready"), sem("qi_hi_done"), sem("qi_lo_done"), sem("ki_hi_done"), sem("ki_lo_done"))
    mt_tr, mt_dve, mt_act, kidx_stored = sem("mt_tr"), sem("mt_dve"), sem("mt_act"), sem("kidx_stored")
    isc_done, isc_relu, isc_added = sem("isc_done"), sem("isc_relu"), sem("isc_added")
    qis_set, pq_done, nw_mm, nw_done, kraw_in = (
        sem("qis_set"), sem("pq_done"), sem("nw_mm"), sem("nw_done"), sem("kraw_in"))
    kid_tr, kis_act, kis_dve, qisb_set, sdots, srelu, ssum, sadd = (
        sem("kid_tr"), sem("kis_act"), sem("kis_dve"), sem("qisb_set"), sem("sdots"), sem("srelu"), sem("ssum"), sem("sadd"))
    k_copied, kv_tr, kv_staged = sem("k_copied"), sem("kv_tr"), sem("kv_staged")
    kv_stored = [sem("kv_stored0"), sem("kv_stored1")]
    idx_ready, idx_tr, rows_ready, snew_ready = sem("idx_ready"), sem("idx_tr"), sem("rows_ready"), sem("snew_ready")
    qh_set, s_mm, p_max, p_exp, p_inv, p_ready, p_tr, pT_ready, pv_mm, pv_out = (
        sem("qh_set"), sem("s_mm"), sem("p_max"), sem("p_exp"), sem("p_inv"), sem("p_ready"), sem("p_tr"),
        sem("pT_ready"), sem("pv_mm"), sem("pv_out"))
    vh_in, st_in, kg_in, vg_in, ridx_set = sem("vh_in"), sem("st_in"), sem("kg_in"), sem("vg_in"), sem("ridx_set")
    qsb_set, qb_mm, km_done, sT_tr, s_max, s_exp, s_ready, sp_tr, pTs_ready, pvs_mm, pvs_out = (
        sem("qsb_set"), sem("qb_mm"), sem("km_done"), sem("sT_tr"), sem("s_max"), sem("s_exp"), sem("s_ready"),
        sem("sp_tr"), sem("pTs_ready"), sem("pvs_mm"), sem("pvs_out"))
    u_ready, u_staged, us_stated, u_stored, state_out = (
        sem("u_ready"), sem("u_staged"), sem("us_stated"), sem("u_stored"), sem("state_out"))
    u_zero, conv_done = sem("u_zero"), sem("conv_done")
    mu_mm, csub, cnorm, csig_done, mix_done, mhi, mlo = (
        sem("mu_mm"), sem("csub"), sem("cnorm"), sem("csig_done"), sem("mix_done"), sem("mhi"), sem("mlo"))
    qlo, kpair_ready = sem("qlo"), sem("kpair_ready")
    x_updated, hb_done, bhi, blo = sem("x_updated"), sem("hb_done"), sem("bhi"), sem("blo")
    g_in, f_tr, f_sum, f_var, f_std, f_y = (
        sem("g_in"), sem("f_tr"), sem("f_sum"), sem("f_var"), sem("f_std"), sem("f_y"))
    y_stored = [sem("y_stored0"), sem("y_stored1")]

    def loop(eng, n, body, first=1, last=0):
        for i in range(min(first, n)):
            body(i)
        if n - first - last == 1:
            body(first)
        elif n - first - last > 1:
            with eng.Fori(first, n - last) as i:
                body(i)
        for i in range(max(n - last, first), n):
            body(i)

    def pick(t, i):
        return t[:, ds(i, 1), :].rearrange("p a n -> p (a n)")

    def pick2(t, i):
        return t[:, ds(i, 1), :].rearrange("p a (h n) -> p (a h) n", h=2)

    def two(t):
        return t.rearrange("p (h n) -> p h n", h=2)

    def pair(T):
        return ps[:, 2 * (T % 2):2 * (T % 2) + 2, 0:NH]


    w_in = a["w_in"].rearrange("l (u k p) n -> p (l u) k n", k=KU, p=P)
    w_out = a["w_out"].rearrange("l (u k p) n -> p (l u) k n", k=KU, p=P)
    w_ff1 = a["w_ff1"].rearrange("l (u k p) n -> p (l u) k n", k=KU, p=P)
    w_ff2 = a["w_ff2"].rearrange("l (b u k p) n -> p (l b) u k n", u=2, k=KU, p=P)
    w_ada = a["w_ada"].rearrange("l (g k p) n -> p (l g) k n", k=4, p=P)
    kidx_pages = a["cache_kidx"].rearrange("l n s d -> (l n) s d")
    cache_k = a["cache_k"].rearrange("l n s h d -> (l n s) (h d)")
    cache_v = a["cache_v"].rearrange("l n s h d -> (l n s) (h d)")
    state = a["state_conv"].rearrange("l (g b) w c -> (l b w) g c", g=2)
    kv_out = [o["k_prompt"].rearrange("l b (t p) h d -> p (l b t) h d", p=P),
              o["v_prompt"].rearrange("l b (t p) h d -> p (l b t) h d", p=P)]
    kvs_out = [o["k_sample"].rearrange("l b s h d -> (l b s) h d"),
               o["v_sample"].rearrange("l b s h d -> (l b s) h d")]

    with nc.Block() as block:

        @block.sync
        def _(sp):
            sp.dma_start(crow[0:1, :], a["c_prompt"]).then_inc(c_in, 16)
            sp.dma_start(crow[1:9, :], a["c_sample"]).then_inc(c_in, 16)
            sp.dma_start(ident[:], a["const_ident"]).then_inc(ident_in, 16)
            at_row = 0
            for name, n in (("norm1_g", KT), ("norm2_g", KT), ("conv_b", CT), ("conv_ln_g", CT), ("conv_ln_b", CT)):
                sp.dma_start(vrow[at_row:at_row + n, :], a[name].rearrange("l (f p) -> (l f) p", p=P)).then_inc(vec_in, 16)
                at_row += n
            sp.dma_start(brow[0:96, :], a["b_ada"].rearrange("l (f p) -> (l f) p", p=P)).then_inc(vec_in, 16)
            sp.dma_start(cwrow[:, :], a["conv_w"].rearrange("l w c -> (l w) c")).then_inc(vec_in, 16)
            sp.dma_start(prow[:], a["page_table"].rearrange("(a b) p -> a (b p)", a=1)).then_inc(pt_in, 16)
            sp.dma_start(xrow[:], a["x_sample"].rearrange("b s d -> (b s) d")).then_inc(xs_in, 16)
            xp = a["x_prompt"].rearrange("b (t p) d -> p (b t) d", p=P)
            for t in range(QT):
                if t >= 2:
                    sp.wait_ge(x_tr, 4 * (t - 1))
                sp.dma_start(xtok[:, t % 2, :], xp[:, t, :]).then_inc(x_in[t % 2], 16)
            sp.dma_start(o["conv_sample"][0, :, 0:W - 2, :], a["state_conv"][0, :, 1:W - 1, :]).then_inc(state_out, 16)

            def load_ada(c):
                for g in range(4):
                    if not isinstance(c, int):
                        sp.wait_ge(ada_lo_done, 4 * (c - 1) + g + 1)
                    sp.dma_start(ada[:, g, :].rearrange("p (k n) -> p k n", k=4), w_ada[:, g, :, ds(c * 512, 512)]
                                 ).then_inc(ada_landed[g], 16)
            loop(sp, ADA_FIRST, load_ada)

            def load(G, src, waits=(0, 1, 2, 3)):
                for uu in range(4):
                    if (not isinstance(G, int) or G >= 1) and waits[uu] is not None:
                        sp.wait_ge(lo_done, 4 * (G - 1) + waits[uu] + 1)
                    sp.dma_start(raw[:, uu, :].rearrange("p (k m) -> p k m", k=KU), src(uu)).then_inc(raw_landed[uu], 16)

            def in_tile(T, col):
                load(T, lambda uu: w_in[:, uu, :, ds(col, P)])

            def ada_pair(c, e, n):
                for g in range(2):
                    if isinstance(n, int) and n > 2 * ADA_OUT:
                        sp.wait_ge(ada_used, 4 * ADA_FIRST + 2 * (n - 1) + g + 1)
                    elif not isinstance(n, int) or n > 0:
                        sp.wait_ge(ada_lo_done, 4 * ADA_FIRST + 2 * (n - 1) + g + 1)
                    sp.dma_start(adl[:, g, :].rearrange("p (k n) -> p k n", k=4), w_ada[:, 2 * e + g, :, ds(c * 512, 512)]
                                 ).then_inc(adl_landed[g], 16)

            in_tile(T_MISC, MISC_COL)
            in_tile(T_QI, 5120)
            in_tile(T_QI + 1, 5120 + P)
            sp.wait_ge(spilled, 16)
            sp.wait_ge(nlo_done, KT + 1)
            for i, name in enumerate(("const_cos", "const_sin", "const_icos", "const_isin")):
                sp.dma_start(rope[:, i, :], a[name]).then_inc(const_in, 16)
            sp.dma_start(caus[:], a["const_future"]).then_inc(const_in, 16)
            sp.dma_start(onehot[:], a["const_onehot"]).then_inc(const_in, 16)
            sp.dma_start(ptab[:], a["page_table"]).then_inc(const_in, 16)
            loop(sp, 6, lambda i: in_tile(T_QI + 2 + i, 5120 + (2 + i) * P), first=0)
            loop(sp, 24, lambda i: in_tile(T_Q + i, 2048 + i * P), first=0)
            def conv_tiles(j):
                in_tile(T_CONV + 2 * j, j * P)
                in_tile(T_CONV + 2 * j + 1, C + j * P)
            conv_tiles(0)

            def conv_loop(j):
                last = isinstance(j, int) and j == CT - 1
                if last:
                    load(T_OUT, lambda uu: w_out[:, (uu + 2) % 4, :, 0:P])
                else:
                    in_tile(T_CONV + 2 * j + 2, (j + 1) * P)
                if isinstance(j, int) and j == 0:
                    sp.wait_ge(kv_stored[0], 32 * 8)
                    sp.wait_ge(kv_stored[1], 32 * 8)
                    sp.wait_ge(idx_tr, 1)
                else:
                    sp.wait_ge(p_tr, j)
                sp.dma_start(st[:], state[:, :, ds(j * P, P)]).then_inc(st_in, 16)
                if not isinstance(j, int) or j > 0:
                    sp.wait_ge(pv_mm, j)
                sp.dma_start(vh[:], kv_out[1][:, :, ds(j, 1), :].rearrange("p t a d -> p t (a d)")).then_inc(vh_in, 16)
                if last:
                    load(T_OUT + 1, lambda uu: w_out[:, (uu + 2) % 4, :, P:2 * P])
                else:
                    in_tile(T_CONV + 2 * j + 3, C + (j + 1) * P)
            loop(sp, CT, conv_loop, last=1)
            sp.wait_ge(s_mm, H)
            ada_pair(ADA_FIRST, 0, 0)
            sp.wait_ge(pvs_out, NS)
            sp.wait_ge(conv_done, CT)
            sp.wait_ge(pT_ready, H)
            sp.wait_ge(pv_mm, H)
            sp.wait_ge(u_stored, 32 * CT)
            sp.dma_start(xT[:].rearrange("p f n -> p (f n)"), xspill).then_inc(reloaded, 16)

            def out_tiles(i):
                for e in range(2):
                    load(T_OUT + 2 + 2 * i + e, lambda uu: w_out[:, (uu + 2) % 4, :, ds((2 + 2 * i + e) * P, P)],
                         waits=(0, 2, None, 3))
                    if not isinstance(i, int) or i > 0:
                        ada_pair(ADA_FIRST + i + e - 1, 1 - e, 2 * i + e - 1)
            loop(sp, KT // 2 - 1, out_tiles)

            def up_tile(b, i):
                load(T_FF + b * 16 + i, lambda uu: w_ff1[:, uu, :, ds((b * FB + i) * P, P)])

            def block_tiles(b, i0):
                with sp.Fori(i0, FB) as i:
                    up_tile(b, i)
                with sp.Fori(0, KT // 2) as i:
                    load(T_FF + b * 16 + 8 + i,
                         lambda uu: w_ff2[:, ds(b, 1), uu % 2, :, ds((2 * i + uu // 2) * P, P)].rearrange("p a k n -> p (a k) n"))
            up_tile(0, 0)
            ada_pair(ADA_FIRST + ADA_OUT - 1, 1, 2 * ADA_OUT - 1)
            up_tile(0, 1)
            for n in range(2 * ADA_GAP):
                ada_pair(ADA_FIRST + ADA_OUT + n // 2, n % 2, 2 * ADA_OUT + n)
            with sp.Fori(0, 1) as b:
                block_tiles(b, 2)
            with sp.Fori(1, BLOCKS) as b:
                block_tiles(b, 0)
            sp.wait_ge(state_out, 16)

        @block.gpsimd
        def _(pool):
            def split_lo(G, gp):
                for uu in range(4):
                    pool.wait_ge(hi_done, 4 * G + uu + 1)
                    nc.gpsimd.tensor_tensor(w_lo[:, 4 * gp + uu, :, :].rearrange("p k m -> p (k m)"), raw[:, uu, :],
                                            w_hi[:, 4 * gp + uu, :, :].rearrange("p k m -> p (k m)").bitcast(F32),
                                            ALU.subtract).then_inc(lo_done, 1)

            def split_pair(G, gp):
                split_lo(G, gp)
                split_lo(G + 1, 1 - gp)

            nc.gpsimd.memset(ones[:], 1.0).then_inc(ones_set, 1)
            pool.wait_ge(pt_in, 16)
            with pool.Fori(0, NS // 2) as m:
                for e in range(2):
                    for page in range(PAGES):
                        r = pool.value_load(prow[0:1, ds(m * (2 * PAGES) + e * PAGES + page, 1)], min_val=0,
                                            max_val=a["cache_kidx"].shape[1] - 1)
                        pool.dma_start(kraw[32 * (page % 4):32 * (page % 4 + 1), ds(m, 1), page // 4, e, :].rearrange("p a d -> p (a d)"),
                                       kidx_pages[ds(r, 1)].rearrange("a (s k) d -> (a s) (k d)", k=4)).then_inc(kraw_in, 16)
            pool.wait_ge(kraw_in, 16 * NS * PAGES)
            for n in range(NS):
                nc.gpsimd.tensor_copy(kpair[:, n // 2, n % 2, :, :, :], kraw[:, n // 2, n % 2, :, :].rearrange(
                    "p e (k d) -> p k e d", k=4)).then_inc(kpair_ready, 1)
            loop(pool, 17, lambda i: split_pair(2 * i, 0), first=0)
            split_lo(34, 0)

            def gathers(j):
                pool.wait_ge(rows_ready, 1)
                if not isinstance(j, int) or j > 0:
                    pool.wait_ge(km_done, j)
                    pool.wait_ge(vg_in, 32 * j)
                nc.gpsimd.tensor_copy(ridx[:], rows[:, :, ds(j, 1)].rearrange("p t a -> p (t a)")).then_inc(ridx_set, 1)
                pool.drain()
                for t in range(2):
                    nc.gpsimd.indirect_dma_start(kg[:, t, :], None, cache_k,
                                                 bass.IndirectOffsetOnAxis(ap=ridx[:, t:t + 1], axis=0)).then_inc(kg_in, 16)
                split_lo(T_CONV + 2 + 2 * j + 1, 0)
                pool.wait_ge(rows_ready, 1)
                if isinstance(j, int) and j == 0:
                    pool.wait_ge(kv_tr, 16)
                else:
                    pool.wait_ge(pvs_mm, j)
                for t in range(2):
                    nc.gpsimd.indirect_dma_start(vg[:, t, :], None, cache_v,
                                                 bass.IndirectOffsetOnAxis(ap=ridx[:, t:t + 1], axis=0)).then_inc(vg_in, 16)

            def conv_loop(j):
                split_lo(T_CONV + 2 + 2 * j, 1)
                gathers(j)
            loop(pool, CT, conv_loop)
            for h in range(H):
                pool.wait_ge(mhi, h + 1)
                nc.gpsimd.tensor_tensor(a_lo[:, CT + h, :], q[:, h, :], a_hi[:, CT + h, :].bitcast(F32), ALU.subtract
                                        ).then_inc(qlo, 1)
            pool.wait_ge(rstd_done, 2)
            for c in range(CT):
                nc.gpsimd.tensor_tensor(conv[:, c, :], conv[:, c, :], rstd[:], ALU.mult).then_inc(cnorm, 1)
            loop(pool, (U_ALL // 4 - 51) // 2, lambda i: split_pair(51 + 2 * i, 1), first=0)

        @block.scalar
        def _(act):
            def copy(out, in_):
                return nc.scalar.activation(out, in_, ACT.Copy)

            def split_hi(G, gp, which=range(4)):
                for uu in which:
                    act.wait_ge(raw_landed[uu], 16 * (G + 1))
                    if not isinstance(G, int) or G >= 2:
                        act.wait_ge(split_used, 4 * G + uu - 7)
                    copy(w_hi[:, 4 * gp + uu, :, :].rearrange("p k m -> p (k m)"), raw[:, uu, :]).then_inc(hi_done, 1)

            act.wait_ge(c_in, 32)
            nc.scalar.activation(csil[:], crow[:], ACT.Sigmoid).then_inc(silu_sig, 1)
            for n in range(1, 4 * QT, 2):
                act.wait_ge(x_tr, n + 1)
                t, g = n // 4, n % 4
                copy(xT[:, 4 * g:4 * g + 4, t * P:(t + 1) * P], ps[:, 4 + n % 4, :].rearrange("p (f n) -> p f n", f=4)
                     ).then_inc(x_copied_act, 1)

            def square(f):
                if f >= 2:
                    act.wait_ge(sq_summed, f - 1)
                nc.scalar.activation(sq[:, f % 2, :], xT[:, f, :], ACT.Square).then_inc(sq_done, 1)

            def std(n):
                act.wait_ge(var_done, n)
                nc.scalar.activation(rstd[:], t1[:, 1, :], ACT.Sqrt).then_inc(std_done, 1)

            def hs_split(n):
                act.wait_ge(hs_done, n)
                copy(a_hi[:, :, NP:N], hs[:]).then_inc(hs_hi, 1)

            def norm_hi(n, shift):
                for f in range(KT):
                    act.wait_ge(t1_done, KT * n + f + 1)
                    nc.scalar.activation(a_hi[:, f, 0:NP], t1[:, f % 2, 0:NP], ACT.Identity,
                                         bias=mod[:, shift + f, 0:1]).then_inc(nhi_done, 1)

            def ada_high(c):
                for g in range(4):
                    if isinstance(c, int) and c < 4 and c + g > 0:
                        square(4 * c + g - 1)
                    act.wait_ge(ada_landed[g], 16 * (c + 1))
                    if not isinstance(c, int) or c > 0:
                        act.wait_ge(ada_used, 4 * c + g - 3)
                    copy(ada_hi[:, g, :], ada[:, g, :]).then_inc(ada_hi_done, 1)

            def ada_rows(c, bank):
                act.wait_ge(ada_used, 4 * (c + 1))
                if not isinstance(c, int) or c > 0:
                    act.wait_ge(ada_tr, c)
                copy(arow[:], ps[0:18, bank, :]).then_inc(ada_row, 1)

            def ada_chunks(i):
                for e in range(2):
                    c = 2 * i + e
                    ada_high(c)
                    if not isinstance(c, int) or c > 0:
                        ada_rows(c - 1, 1 - e)
            act.wait_ge(x_copied_dve, 9)
            ada_chunks(0)
            ada_chunks(1)
            square(KT - 1)
            std(1)
            ada_chunks(2)
            for m in range(NS // 2):
                act.wait_ge(kid_tr, 2 * m + 2)
                copy(kisT[:, m, 512:1024].rearrange("p (s k) -> p s k", k=4),
                     ps[:, 5, :].rearrange("p (k s) -> p s k", k=4)).then_inc(kis_act, 1)
            loop(act, ADA_FIRST // 2 - 3, lambda i: ada_chunks(3 + i), first=0)
            ada_high(ADA_FIRST - 1)
            ada_rows(ADA_FIRST - 2, 1)
            split_hi(0, 0)
            ada_rows(ADA_FIRST - 1, 0)
            split_hi(1, 1)
            act.dma_start(xspill, xT[:].rearrange("p f n -> p (f n)")).then_inc(spilled, 16)
            act.wait_ge(ada_used, 4 * ADA_FIRST)
            hs_split(1)
            norm_hi(0, 0)

            def swap(T, tp, step):
                act.wait_ge(split_used, 4 * (T + 1))
                if not isinstance(T, int) or T >= 2:
                    act.wait_ge(free_dve, T - 1)
                for p0 in range(0, P, 2 * step):
                    copy(two(sw[p0:p0 + step, tp, :]), pair(tp)[p0 + step:p0 + 2 * step])
                    last = copy(two(sw[p0 + step:p0 + 2 * step, tp, :]), pair(tp)[p0:p0 + step])
                last.then_inc(swapped, 1)

            split_hi(T_MISC + 2, 0)
            act.wait_ge(split_used, 4 * (T_MISC + 1))
            act.wait_ge(spilled, 16)
            act.wait_ge(nlo_done, KT + 1)
            copy(two(wiT[:]), pair(T_MISC)[DI:DI + HI]).then_inc(wi_ready, 1)
            copy(two(sw[0:32, 0, :]), pair(T_MISC)[32:64])
            copy(two(sw[32:64, 0, :]), pair(T_MISC)[0:32]).then_inc(swapped, 1)
            act.wait_ge(free_dve, T_MISC + 1)
            copy(ki_hi[0:DI, :], kiT[:, 0:NP])
            copy(ki_hi[DI:P, :], kiT[:, 0:NP]).then_inc(ki_hi_done, 1)

            def index_relu(m):
                for n in range(6 * m, 6 * m + 6):
                    act.wait_ge(isc_done, n + 1)
                    if n >= 2:
                        act.wait_ge(isc_added, n - 1)
                    w = (n % 3 + 2) * P
                    nc.scalar.activation(rs[:, n % 2, 0:w], ps[:, 4 + n % 2, 0:w], ACT.Relu, scale=DI ** -0.5).then_inc(isc_relu, 1)

            for m in range(HI // 2):
                T, tp, e = T_QI + m, (T_QI + m) % 2, m % 2
                swap(T, tp, 32)
                if m == 1:
                    act.wait_ge(mt_tr, 1)
                    copy(kio[:, 0:QT * DI], ps[:, 6, 0:QT * DI])
                    copy(kio[0:NS, QT * DI:], ps[0:NS, 7, 0:DI]).then_inc(mt_act, 1)
                    act.wait_ge(mt_act, 1)
                    act.dma_start(o["kidx_prompt"].rearrange("l b (t p) d -> p (l b t) d", p=P),
                                  kio[:, 0:QT * DI].rearrange("p (t d) -> p t d", d=DI)).then_inc(kidx_stored, 16)
                    act.dma_start(o["kidx_sample"].rearrange("l b s d -> (l b s) d"), kio[0:NS, QT * DI:]).then_inc(kidx_stored, 16)
                split_hi(T + 2, tp)
                act.wait_ge(free_dve, T + 1)
                copy(qiw[e][0:DI, m // 2 * 2, :], kv[0:DI, tp, P:NP])
                copy(qiw[e][DI:P, m // 2 * 2 + 1, :], kv[DI:P, tp, P:NP]).then_inc(qi_hi_done, 1)
                if m == HI // 2 - 1:
                    act.wait_ge(qi_lo_done, HI // 2)
                    copy(qis[:].rearrange("p (m e) b -> p m e b", e=2)[:, :, 0, :], qid[0:DI, :, :])
                    copy(qis[:].rearrange("p (m e) b -> p m e b", e=2)[:, :, 1, :], qid[DI:P, :, :]).then_inc(qis_set, 1)
                if m >= 1:
                    index_relu(m - 1)

            def q_body(i):
                for e in range(2):
                    b = 2 * i + e
                    T, tp = T_Q + b, (T_Q + e) % 2
                    if isinstance(i, int) and b == 0:
                        act.wait_ge(pq_done, 1)
                    else:
                        act.wait_ge(ssum, b)
                    copy(qisb[e * DI:(e + 1) * DI, e, :], qis[:, :, ds(b, 1)].rearrange("p h a -> p (h a)"))
                    copy(wib[:], wisel[:, ds(b, 1), :].rearrange("p a n -> p (a n)")).then_inc(qisb_set, 1)
                    act.wait_ge(sdots, b + 1)
                    for c in range(2):
                        last = nc.scalar.activation(rsd[:, c, :], ps[0:HI, 6 + c, :], ACT.Relu, scale=DI ** -0.5)
                    last.then_inc(srelu, 1)
                    swap(T, tp, 64)
                    split_hi(T + 2, tp)
                    if isinstance(i, int) and b == 0:
                        index_relu(HI // 2 - 1)
                        act.wait_ge(kidx_stored, 32)
            loop(act, 4, q_body)

            def kv_flush(n, slot, out, out_s, h):
                act.wait_ge(kv_tr, n + 1)
                if not isinstance(n, int) or n >= 2:
                    act.wait_ge(kv_stored[slot], 16 * (n - slot))
                copy(kvst[:, slot, :], ps[:, 4, :])
                copy(kvsts[:, slot, :], ps[0:NS, 5, 0:P]).then_inc(kv_staged, 1)
                act.wait_ge(kv_staged, n + 1)
                act.dma_start(out[:, :, ds(h, 1), :].rearrange("p t a d -> p t (a d)"),
                              kvst[:, slot, :].rearrange("p (t d) -> p t d", d=P)).then_inc(kv_stored[slot], 16)
                act.dma_start(out_s[:, ds(h, 1), :].rearrange("p a d -> p (a d)"), kvsts[:, slot, :]).then_inc(kv_stored[slot], 16)

            def k_body(i):
                for e in range(2):
                    n = 2 * i + e
                    T, tp = T_K + n, (T_K + e) % 2
                    if not (isinstance(i, int) and n == 0):
                        kv_flush(n - 1, 1 - e, kv_out[0], kvs_out[0], n - 1)
                    swap(T, tp, 64)
                    split_hi(T + 2, tp)
                    act.wait_ge(free_dve, T + 1)
                    copy(pick(k, n), kv[:, tp, :]).then_inc(k_copied, 1)
            loop(act, 4, k_body)

            def v_body(i):
                for e in range(2):
                    n = 2 * i + e
                    T, tp = T_V + n, (T_V + e) % 2
                    if isinstance(i, int) and n == 0:
                        kv_flush(7, 1, kv_out[0], kvs_out[0], 7)
                    else:
                        kv_flush(8 + n - 1, 1 - e, kv_out[1], kvs_out[1], n - 1)
                    act.wait_ge(split_used, 4 * (T + 1))
                    act.wait_ge(kv_tr, 8 + n - 1)
                    copy(two(kv[:, tp, :]), pair(tp))
                    copy(vs[:, ds(n, 1), :].rearrange("p a n -> p (a n)"),
                         pair(tp)[:, 1, NH - NS:NH]).then_inc(free_act, 1)
                    split_hi(T + 2, tp)
            loop(act, 4, v_body)

            def head_out(jj):
                act.wait_ge(pv_mm, jj + 1)
                copy(q[:, ds(jj, 1), 0:NP].rearrange("p a n -> p (a n)"), ps[:, 7, :]).then_inc(pv_out, 1)

            def row_exp(jj):
                act.wait_ge(s_max, jj + 1)
                nc.scalar.activation(sm[:], sm[:], ACT.Exp, bias=ssm[:, 1:2], accum_out=ssm[:, 2:3]).then_inc(s_exp, 1)

            def row_p(jj):
                act.wait_ge(sp_tr, jj + 1)
                copy(pTs[:], ps[:, 6, 256:272].rearrange("p (t h) -> p t h", t=2)).then_inc(pTs_ready, 1)

            def store_u(jj):
                copy(ost[0:W - 1, :], ps[0:W - 1, 7, 384:512])
                copy(ost[32:32 + NS, :], ps[0:NS, 5, 384:512]).then_inc(u_staged, 1)
                act.wait_ge(u_staged, jj + 1)
                act.dma_start(o["conv_prompt"].rearrange("l b w c -> (l b w) c")[:, ds(jj * P, P)], ost[0:W - 1, :]
                              ).then_inc(u_stored, 16)
                act.dma_start(o["conv_sample"].rearrange("l b w c -> b (l w) c")[:, W - 2, ds(jj * P, P)], ost[32:32 + NS, :]
                              ).then_inc(u_stored, 16)

            def conv_body(j):
                first = isinstance(j, int) and j == 0
                Ta, pa = T_CONV + 2 * j, T_CONV % 2
                if first:
                    kv_flush(15, 1, kv_out[1], kvs_out[1], 7)
                    act.wait_ge(idx_tr, 1)
                    act.wait_ge(kv_stored[0], 32 * 8)
                    act.wait_ge(kv_stored[1], 32 * 8)
                else:
                    act.wait_ge(s_mm, j)
                copy(qh[:], pick(q, j)).then_inc(qh_set, 1)
                if not first:
                    act.wait_ge(qb_mm, j)
                copy(qsb[:], q[:, :, ds(NP + j, 1)].rearrange("p h a -> p (h a)")).then_inc(qsb_set, 1)
                split_hi(Ta + 2, pa, range(2))
                if not first:
                    head_out(j - 1)
                split_hi(Ta + 2, pa, range(2, 4))
                if not first:
                    row_exp(j - 1)
                act.wait_ge(split_used, 4 * (Ta + 1))
                if not first:
                    act.wait_ge(u_ready, j)
                copy(two(ua[:]), pair(pa)).then_inc(free_act, 1)
                split_hi(Ta + 3, 1 - pa, range(1))
                act.wait_ge(p_max, j + 1)
                for t in range(QT):
                    lo, w = t * (t + 1) // 2 * P, (t + 1) * P
                    last = nc.scalar.activation(pr[:, lo:lo + w], pr[:, lo:lo + w], ACT.Exp, bias=pm[:, 4 + t:5 + t],
                                                accum_out=pm[:, 8 + t:9 + t])
                last.then_inc(p_exp, 1)
                if not first:
                    row_p(j - 1)
                split_hi(Ta + 3, 1 - pa, range(1, 2))
                act.wait_ge(p_inv, j + 1)
                for t in range(QT):
                    lo, w = t * (t + 1) // 2 * P, (t + 1) * P
                    last = nc.scalar.activation(pr[:, lo:lo + w], pr[:, lo:lo + w], ACT.Copy, scale=pm[:, 12 + t:13 + t])
                last.then_inc(p_ready, 1)
                split_hi(Ta + 3, 1 - pa, range(2, 4))
                act.wait_ge(split_used, 4 * (Ta + 2))
                nc.scalar.activation(two(sg[:]), pair(1 - pa), ACT.Sigmoid).then_inc(free_act, 1)
                act.wait_ge(p_tr, j + 1)
                copy(pr[:, 0:512], ps[:, 4, :])
                copy(pr[:, 512:896], ps[:, 5, 0:384])
                copy(pr[:, 896:1280], ps[:, 7, 0:384]).then_inc(pT_ready, 1)
                if not first:
                    if not isinstance(j, int):
                        act.wait_ge(u_stored, 32 * (j - 1))
                    store_u(j - 1)
            loop(act, CT, conv_body, first=2)
            head_out(7)
            row_exp(7)
            row_p(7)
            act.wait_ge(p_tr, CT + 1)
            act.wait_ge(u_stored, 32 * 7)
            store_u(7)

            act.wait_ge(pvs_out, NS)
            for h in range(H):
                copy(a_hi[:, CT + h, :], q[:, h, :]).then_inc(mhi, 1)
            for c in range(CT):
                act.wait_ge(csub, c + 1)
                act.wait_ge(sq_summed, KT + c - 1)
                nc.scalar.activation(sq[:, c % 2, :], conv[:, c, :], ACT.Square).then_inc(sq_done, 1)
            std(2)
            for c in range(CT):
                act.wait_ge(cnorm, c + 1)
                if c >= 2:
                    act.wait_ge(mix_done, c - 1)
                nc.scalar.activation(sq[:, c % 2, :], conv[:, c, :], ACT.Identity, scale=vec[:, 40 + c:41 + c],
                                     bias=vec[:, 48 + c:49 + c])
                nc.scalar.activation(t1[:, c % 2, :], conv[:, c, :], ACT.Sigmoid, scale=vec[:, 40 + c:41 + c],
                                     bias=vec[:, 48 + c:49 + c]).then_inc(csig_done, 1)
                if c >= 1:
                    act.wait_ge(mix_done, c)
                    copy(a_hi[:, c - 1, :], conv[:, c - 1, :]).then_inc(mhi, 1)
            act.wait_ge(mix_done, CT)
            copy(a_hi[:, CT - 1, :], conv[:, CT - 1, :]).then_inc(mhi, 1)

            def ada_beside(i, e):
                for g in range(2):
                    act.wait_ge(adl_landed[g], 16 * (2 * i + e - 1))
                    act.wait_ge(ada_used, 4 * (ADA_FIRST + i - 1) + 2 * e + g - 1)
                    copy(adl_hi[:, g, :], adl[:, g, :]).then_inc(ada_hi_done, 1)

            def out_body(i):
                for e in range(2):
                    T, tp = T_OUT + 2 * i + e, (T_OUT + e) % 2
                    if e == 0 and (not isinstance(i, int) or i > 1):
                        ada_rows(ADA_FIRST + i - 2, 4)
                    if not isinstance(i, int) or i > 0:
                        ada_beside(i, e)
                    else:
                        act.wait_ge(qlo, H)
                    split_hi(T + 2, tp)
                    act.wait_ge(x_updated, 2 * i + e + 1)
                    act.wait_ge(sq_summed, KT + CT + 2 * i + e - 1)
                    nc.scalar.activation(sq[:, e, :], pick(xT, 2 * i + e), ACT.Square).then_inc(sq_done, 1)
            loop(act, KT // 2, out_body, first=2)
            ada_rows(ADA_FIRST + ADA_OUT - 1, 4)
            std(3)
            hs_split(2)
            norm_hi(1, 48)
            ada_rows(22, 4)
            ada_rows(23, 6)

            def block_body(b, last=False):
                def up(i):
                    for e in range(2):
                        n = 2 * i + e
                        split_hi(T_FF + b * 16 + n + 2, (T_FF + e) % 2)
                        act.wait_ge(hb_done, b * FB + n + 1)
                        copy(pick(b_hi, n), t1[:, e, :]).then_inc(bhi, 1)
                loop(act, FB // 2, up, first=0)

                def down(i):
                    for e in range(2):
                        split_hi(T_FF + b * 16 + 8 + 2 * i + e + 2, (T_FF + e) % 2)
                loop(act, FB // 2 - int(last), down, first=0)
            with act.Fori(0, BLOCKS - 1) as b:
                block_body(b)
            block_body(BLOCKS - 1, last=True)

            act.dma_start(grow[:], a["final_g"].rearrange("(a n) -> a n", a=1).broadcast_to([P, D])).then_inc(g_in, 16)
            for t in range(QT + 2):
                if t <= QT:
                    n = P if t < QT else NS
                    act.wait_ge(f_tr, t + 1)
                    nc.scalar.activation(fsq[0:n, :], ps[0:n, 4 * (t % 2):4 * (t % 2) + 4, :].rearrange("p a n -> p (a n)"),
                                         ACT.Square, accum_out=fstat[0:n, t, 0:1]).then_inc(f_sum, 1)
                    act.wait_ge(f_var, t + 1)
                    nc.scalar.activation(fstat[0:n, t, 2:3], fstat[0:n, t, 1:2], ACT.Sqrt).then_inc(f_std, 1)
                if t >= 1:
                    s = t - 1
                    n = P if s < QT else NS
                    act.wait_ge(f_y, s + 1)
                    act.dma_start((o["y_prompt"].rearrange("b (t p) d -> p (b t) d", p=P)[:, s, :] if s < QT
                                   else o["y_sample"].rearrange("b s d -> (b s) d")),
                                  yrow[0:n, s % 2, :]).then_inc(y_stored[s % 2], 16)
            act.wait_ge(y_stored[0], 48)
            act.wait_ge(y_stored[1], 32)
            act.wait_ge(spilled, 16)

        @block.vector
        def _(dve):
            V = nc.vector
            dve.wait_ge(c_in, 32)
            dve.wait_ge(silu_sig, 1)
            V.tensor_tensor(csil[:], csil[:], crow[:], ALU.mult).then_inc(silu_done, 1)
            dve.wait_ge(c_tr, 1)
            c_ps = ps[:, 0, 0:KT * 9].rearrange("p (k n) -> p k n", n=9)
            V.tensor_copy(cT[:, :, 0:9], c_ps)
            dve.drain()
            V.tensor_tensor(cT[:, :, 9:18], c_ps, cT[:, :, 0:9].bitcast(F32), ALU.subtract).then_inc(c_ready, 1)
            dve.wait_ge(vec_tr, 1)
            V.tensor_copy(vec[:], ps[:, 1, 0:56])
            V.tensor_copy(bada[:], ps[:, 2, 0:96])
            V.tensor_copy(cw[:, :, 0:W], ps[:, 3, 0:CT * W].rearrange("p (c w) -> p c w", c=CT))
            dve.drain()
            V.tensor_copy(cw[:, :, W], vec[:, 32:40]).then_inc(vec_ready, 1)
            for n in range(0, 4 * QT, 2):
                dve.wait_ge(x_tr, n + 1)
                t, g = n // 4, n % 4
                V.tensor_copy(xT[:, 4 * g:4 * g + 4, t * P:(t + 1) * P], ps[:, 4 + n % 4, :].rearrange("p (f n) -> p f n", f=4)
                              ).then_inc(x_copied_dve, 1)
            dve.wait_ge(x_tr, 4 * QT + 1)
            V.tensor_copy(xT[:, :, NP:N], ps[:, 4, 0:KT * NS].rearrange("p (f n) -> p f n", f=KT)).then_inc(x_copied_dve, 1)

            def inv_std(n, width):
                dve.wait_ge(sq_summed, (KT, KT + CT, 2 * KT + CT)[n - 1])
                V.tensor_scalar(two(t1[:, 1, :]), ps[:, 6:8, 0:NH], 1.0 / width, EPS, ALU.mult, ALU.add).then_inc(var_done, 1)
                dve.wait_ge(std_done, n)
                V.reciprocal(rstd[:], rstd[:])
                dve.drain()
                V.scalar_tensor_tensor(sq[:, 0, :], rstd[:], -0.5, rstd[:], ALU.mult, ALU.mult)
                dve.drain()
                V.tensor_tensor(sq[:, 0, :], sq[:, 0, :], t1[:, 1, :], ALU.mult)
                dve.drain()
                V.scalar_tensor_tensor(rstd[:], sq[:, 0, :], 1.5, rstd[:], ALU.add, ALU.mult).then_inc(rstd_done, 1)
                dve.drain()

            def ada_low(c):
                for g in range(4):
                    dve.wait_ge(ada_hi_done, 4 * c + g + 1)
                    if not isinstance(c, int) or 4 * c + g >= 2:
                        dve.wait_ge(ada_used, 4 * c + g - 1)
                    V.tensor_tensor(ada_lo[:, g % 2, :], ada[:, g, :], ada_hi[:, g, :].bitcast(F32), ALU.subtract
                                    ).then_inc(ada_lo_done, 1)

            def mods(c, bank):
                dve.wait_ge(ada_tr, c + 1)
                parts = ps[:, bank, 0:72].rearrange("p (f n) -> p f n", f=4)
                V.tensor_copy(mod[:, ds(4 * c, 4), :], parts[:, :, 0:9])
                dve.drain()
                V.tensor_tensor(mod[:, ds(4 * c, 4), :], mod[:, ds(4 * c, 4), :], parts[:, :, 9:18], ALU.add).then_inc(mod_done, 1)

            def ada_chunks(i):
                for e in range(2):
                    ada_low(2 * i + e)
                    if not isinstance(i, int) or i > 0:
                        mods(2 * i + e - 2, 2 + e)

            def add_bias(f0, f1):
                V.tensor_tensor(mod[:, f0:f1, :], mod[:, f0:f1, :], bada[:, f0:f1].unsqueeze(2).broadcast_to([P, f1 - f0, 9]), ALU.add)
                dve.drain()

            def gains(n):
                V.scalar_tensor_tensor(gain[:, n, :, :], mod[:, 16 + 48 * n:32 + 48 * n, :], 1.0,
                                       vec[:, 16 * n:16 * n + 16].unsqueeze(2).broadcast_to([P, KT, 9]), ALU.add, ALU.mult)
                dve.drain()
            ada_chunks(0)
            ada_chunks(1)
            inv_std(1, D)
            ada_chunks(2)
            for m in range(NS // 2):
                dve.wait_ge(kid_tr, 2 * m + 1)
                V.tensor_copy(kisT[:, m, 0:512].rearrange("p (s k) -> p s k", k=4),
                              ps[:, 4, :].rearrange("p (k s) -> p s k", k=4)).then_inc(kis_dve, 1)
            loop(dve, ADA_FIRST // 2 - 3, lambda i: ada_chunks(3 + i), first=0)
            ada_low(ADA_FIRST - 1)
            mods(ADA_FIRST - 3, 2)
            dve.drain()
            add_bias(0, 32)
            gains(0)

            def normed(n, shift, between=None):
                V.tensor_tensor(hs[:], xT[:, :, NP:N], rstd[:, NP:N].unsqueeze(1).broadcast_to([P, KT, NS]), ALU.mult)
                dve.drain()
                V.tensor_tensor(hs[:], hs[:], gain[:, n, :, 1:9], ALU.mult)
                dve.drain()
                V.tensor_tensor(hs[:], hs[:], mod[:, shift:shift + KT, 1:9], ALU.add).then_inc(hs_done, 1)

                dve.drain()

                def scaled(f):
                    if f >= 2:
                        dve.wait_ge(nlo_done, (KT + 1) * n + f)
                    if n or f >= 2:
                        dve.wait_ge(nhi_done, KT * n + max(f - 1, 0))
                    V.scalar_tensor_tensor(t1[:, f % 2, 0:NP], xT[:, f, 0:NP], gain[:, n, f, 0:1], rstd[:, 0:NP],
                                           ALU.mult, ALU.mult).then_inc(t1_done, 1)

                def low(f):
                    dve.wait_ge(nhi_done, KT * n + f + 1)
                    V.scalar_tensor_tensor(a_lo[:, f, 0:NP], t1[:, f % 2, 0:NP], mod[:, shift + f, 0:1],
                                           a_hi[:, f, 0:NP].bitcast(F32), ALU.add, ALU.subtract).then_inc(nlo_done, 1)
                scaled(0)
                if between is not None:
                    between()
                dve.wait_ge(hs_hi, n + 1)
                V.tensor_tensor(a_lo[:, :, NP:N], hs[:], a_hi[:, :, NP:N].bitcast(F32), ALU.subtract).then_inc(nlo_done, 1)
                for f in range(KT):
                    if f + 1 < KT:
                        scaled(f + 1)
                    low(f)
            dve.wait_ge(ada_used, 4 * ADA_FIRST)
            normed(0, 0, lambda: (mods(ADA_FIRST - 2, 3), mods(ADA_FIRST - 1, 2)))
            add_bias(32, 4 * ADA_FIRST)

            def rotate(T, tp, cos, out):
                dve.wait_ge(swapped, T + 1)
                V.tensor_tensor(two(kv[:, tp, :]), pair(tp), two(rope[:, cos, :]), ALU.mult)
                V.tensor_tensor(sw[:, tp, :], sw[:, tp, :], rope[:, cos + 1, :], ALU.mult)
                dve.drain()
                V.tensor_tensor(out, kv[:, tp, :], sw[:, tp, :], ALU.add).then_inc(free_dve, 1)

            dve.wait_ge(const_in, 112)

            dve.wait_ge(swapped, T_MISC + 1)
            V.tensor_tensor(two(kv[0:DI, 0, :]), pair(T_MISC)[0:DI], two(rope[0:DI, 2, :]), ALU.mult)
            V.tensor_tensor(sw[0:DI, 0, :], sw[0:DI, 0, :], rope[0:DI, 3, :], ALU.mult)
            dve.drain()
            V.tensor_tensor(kiT[:], kv[0:DI, 0, :], sw[0:DI, 0, :], ALU.add).then_inc(free_dve, 1)
            dve.wait_ge(ki_hi_done, 1)
            V.tensor_tensor(ki_lo[0:DI, :], kiT[:, 0:NP], ki_hi[0:DI, :].bitcast(F32), ALU.subtract)
            V.tensor_tensor(ki_lo[DI:P, :], kiT[:, 0:NP], ki_hi[0:DI, :].bitcast(F32), ALU.subtract).then_inc(ki_lo_done, 1)
            V.memset(qisb[DI:P, 0, :], 0.0)
            V.memset(qisb[0:DI, 1, :], 0.0)
            dve.wait_ge(wi_ready, 1)
            V.tensor_tensor(wisel[:], onehot[:], wiT[:, NP:N].unsqueeze(1).broadcast_to([HI, NS, NS]), ALU.mult)
            dve.drain()
            V.tensor_scalar(wisel[:], wisel[:], HI ** -0.5, None, ALU.mult)
            off = [0, P, 3 * P, 6 * P]

            def index_add(m):
                for n in range(6 * m, 6 * m + 6):
                    t, h = n % 3 + 1, n // 3
                    w = (t + 1) * P
                    dve.wait_ge(isc_relu, n + 1)
                    s_t = sc[:, off[t]:off[t] + w]
                    if h == 0:
                        V.tensor_scalar(s_t, rs[:, n % 2, 0:w], wtok[:, t, h:h + 1], None, ALU.mult).then_inc(isc_added, 1)
                    else:
                        V.scalar_tensor_tensor(s_t, rs[:, n % 2, 0:w], wtok[:, t, h:h + 1], s_t, ALU.mult, ALU.add
                                               ).then_inc(isc_added, 1)
                    if t == 3:
                        dve.drain()

            for m in range(HI // 2):
                T, tp = T_QI + m, (T_QI + m) % 2
                rotate(T, tp, 2, kv[:, tp, :])
                if m == 1:
                    dve.wait_ge(mt_tr, 1)
                    V.tensor_scalar(wtok[:], ps[:, 4, 0:QT * HI].rearrange("p (t h) -> p t h", t=QT), HI ** -0.5, None, ALU.mult)
                    V.tensor_scalar(wis8[:], ps[0:NS, 5, 0:HI], HI ** -0.5, None, ALU.mult).then_inc(mt_dve, 1)
                dve.wait_ge(qi_hi_done, m + 1)
                for half in range(2):
                    top, other = slice(half * DI, half * DI + DI), slice(DI - half * DI, P - half * DI)
                    w = qiw[m % 2][:, m // 2 * 2 + half, :]
                    V.tensor_tensor(w[other], kv[top, tp, P:NP], w[top].bitcast(F32), ALU.subtract)
                V.tensor_copy(qid[:, m, :], kv[:, tp, NP:N]).then_inc(qi_lo_done, 1)
                dve.drain()
                if m == HI // 2 - 1:
                    dve.wait_ge(qis_set, 1)
                    V.tensor_tensor(pq[0:DI, :, :], qis[:], kiT[0:DI, NP:N].unsqueeze(1).broadcast_to([DI, HI, NS]), ALU.mult
                                    ).then_inc(pq_done, 1)
                if m >= 1:
                    index_add(m - 1)
            dve.wait_ge(nw_mm, 1)
            V.tensor_scalar(nw[:], ps[0:NS, 6, 0:HI * NS], DI ** -0.5, 0.0, ALU.mult, ALU.max).then_inc(nw_done, 1)
            dve.drain()
            nw3 = nw[:].rearrange("p (h b) -> p h b", h=HI)
            V.tensor_tensor(nw3, nw3, wis8[:].unsqueeze(2).broadcast_to([NS, HI, NS]), ALU.mult)
            dve.drain()
            V.tensor_tensor(nw3, nw3, ident[0:NS, 0:NS].unsqueeze(1).broadcast_to([NS, HI, NS]), ALU.mult)
            dve.drain()
            V.tensor_reduce(ssc[:, PAST:NK], nw[:], AX, ALU.add)

            def index_done():
                index_add(HI // 2 - 1)
                for t in range(1, QT):
                    diag = sc[:, off[t] + t * P:off[t] + (t + 1) * P]
                    V.tensor_tensor(diag, diag, caus[:], ALU.add)
                V.tensor_scalar(sc[:, 0:P], caus[:], MASKED / FUTURE, None, ALU.mult)
                dve.drain()

            def top_prompt():
                for t in range(1, QT):
                    V.max(m8[:, t, :], sc[:, off[t]:off[t] + (t + 1) * P])
                dve.drain()
                for t in range(1, QT):
                    s_t = sc[:, off[t]:off[t] + (t + 1) * P]
                    V.match_replace(s_t, m8[:, t, :], s_t, TAKEN)
                dve.drain()

            def q_body(i):
                for e in range(2):
                    b = 2 * i + e
                    T, tp = T_Q + b, (T_Q + e) % 2
                    rotate(T, tp, 0, pick(q, b))
                    dve.wait_ge(ssum, b + 1)
                    if isinstance(i, int) and b == 0:
                        V.tensor_copy(ssc[:, 0:512], ps[0:NS, 6, :])
                        V.tensor_copy(ssc[:, 512:1024], ps[0:NS, 7, :]).then_inc(sadd, 1)
                    else:
                        V.tensor_tensor(ssc[:, 0:512], ssc[:, 0:512], ps[0:NS, 6, :], ALU.add)
                        V.tensor_tensor(ssc[:, 512:1024], ssc[:, 512:1024], ps[0:NS, 7, :], ALU.add).then_inc(sadd, 1)
                    dve.drain()
                    if isinstance(i, int) and i == 0:
                        if e == 0:
                            index_done()
                    else:
                        for _ in range(3 - e):
                            top_prompt()
            loop(dve, 4, q_body)
            top_prompt()
            V.tensor_scalar(sc[:, P:], sc[:, P:], TAKEN_BELOW, MASKED, ALU.is_gt, ALU.mult)

            def top_rows(r):
                V.max(m8[0:NS, 0, :], ssc[:, 0:NK])
                dve.drain()
                V.max_index(i8[:, 0, :], m8[0:NS, 0, :], ssc[:, 0:NK])
                dve.drain()
                V.match_replace(ssc[:, 0:NK], m8[0:NS, 0, :], ssc[:, 0:NK], TAKEN)
                V.tensor_copy(sidx[:, ds(r * 8, 8)], i8[:, 0, :])
                dve.drain()

            def k_body(i):
                for e in range(2):
                    n = 2 * i + e
                    T, tp = T_K + n, (T_K + e) % 2
                    if not isinstance(i, int):
                        dve.wait_ge(kv_tr, n - 1)
                        dve.wait_ge(k_copied, n - 1)
                    rotate(T, tp, 0, kv[:, tp, :])
                    top_rows(2 * n)
                    top_rows(2 * n + 1)
            loop(dve, 4, k_body)
            loop(dve, 16, lambda r: top_rows(16 + r), first=0)

            V.tensor_copy(ptf[:], ptab[:])
            V.tensor_copy(iu[:, 0, :], sidx[:, 0:TOPS])
            dve.drain()
            V.tensor_scalar(iu[:, 1, :], iu[:, 0, :], 7, None, ALU.logical_shift_right)
            dve.drain()
            V.tensor_copy(fi[:, 0, :], iu[:, 1, :])
            dve.drain()
            V.scalar_tensor_tensor(fi[:, 1, :], fi[:, 0, :], -float(PAGE), sidx[:, 0:TOPS], ALU.mult, ALU.add)
            V.tensor_scalar(fi[:, 2, :], sidx[:, 0:TOPS], float(PAST), None, ALU.is_ge)
            for page in range(PAGES):
                V.tensor_scalar(fi[:, 3, :], fi[:, 0, :], float(page), ptf[:, page:page + 1], ALU.is_equal, ALU.mult)
                dve.drain()
                V.scalar_tensor_tensor(fi[:, 1, :], fi[:, 3, :], float(PAGE), fi[:, 1, :], ALU.mult, ALU.add)
                dve.drain()
            V.reduce_max(ssc[:, 0:1], fi[:, 2, :], AX)
            dve.wait_ge(k_copied, H)
            V.tensor_tensor(pq[:, 0:H, :], q[:, :, NP:N], k[:, :, NP:N], ALU.mult).then_inc(idx_ready, 1)
            dve.wait_ge(idx_tr, 1)
            V.tensor_copy(rows[:], ps[:, 6, 0:16].rearrange("p (t b) -> p t b", t=2)).then_inc(rows_ready, 1)
            V.tensor_scalar(smask[:], ps[:, 6, 16:32].rearrange("p (t b) -> p t b", t=2), MASKED, None, ALU.mult)
            V.tensor_scalar(snew[:], ps[0:H, 6, 40:48], -MASKED, MASKED, ALU.mult, ALU.add)
            dve.drain()
            V.scalar_tensor_tensor(snew[:], ps[0:H, 6, 32:40], SCALE, snew[:], ALU.mult, ALU.add).then_inc(snew_ready, 1)

            dve.wait_ge(kv_stored[0], 32 * 8)
            dve.wait_ge(kv_stored[1], 32 * 8)
            V.memset(u[:, 0:W - 1], 0.0).then_inc(u_zero, 1)
            dve.drain()

            def taps(k0, k1):
                for w in range(k0, k1):
                    if w < 2:
                        V.tensor_scalar(acc[:, w, :], u[:, w:w + NP], cwb[:, w:w + 1], None, ALU.mult)
                    else:
                        V.scalar_tensor_tensor(acc[:, w % 2, :], u[:, w:w + NP], cwb[:, w:w + 1], acc[:, w % 2, :],
                                               ALU.mult, ALU.add)
                    if w % 2:
                        dve.drain()

            def lag_scores(jj):
                dve.wait_ge(qb_mm, jj + 1)
                dve.wait_ge(kg_in, 32 * (jj + 1))
                for t in range(2):
                    V.tensor_tensor(kg[:, t, :], kg[:, t, :], ps[:, 4:6, :].rearrange("p a n -> p (a n)"), ALU.mult)
                V.tensor_copy(cwb[:], pick(cw, jj))
                dve.drain()
                V.tensor_reduce(sT[:], kg[:].rearrange("p t (h d) -> p t h d", h=H), AX, ALU.add)
                dve.drain()
                for t in range(2):
                    last = V.tensor_scalar(sT[:, t, :], sT[:, t, :], SCALE, smask[:, t, ds(jj, 1)], ALU.mult, ALU.add)
                last.then_inc(km_done, 1)

            def lag_softmax(jj):
                dve.wait_ge(sT_tr, jj + 1)
                V.tensor_copy(sm[:, 0:TOPS], ps[0:H, 6, 0:TOPS])
                V.tensor_copy(sm[:, TOPS:TOPS + 1], snew[:, ds(jj, 1)])
                dve.drain()
                V.reduce_max(ssm[:, 0:1], sm[:], AX)
                dve.drain()
                V.tensor_scalar(ssm[:, 1:2], ssm[:, 0:1], -1.0, None, ALU.mult).then_inc(s_max, 1)

            def lag_weights(jj):
                dve.wait_ge(s_exp, jj + 1)
                V.reciprocal(ssm[:, 3:4], ssm[:, 2:3])
                dve.drain()
                V.tensor_scalar(sm[:], sm[:], ssm[:, 3:4], None, ALU.mult)
                dve.drain()
                V.tensor_scalar(dg[:], ident[0:H, 0:H], sm[:, TOPS:TOPS + 1], None, ALU.mult).then_inc(s_ready, 1)

            def lag_rest(jj, k0=12, k1=26):
                taps(k0, k1)
                dve.wait_ge(pvs_mm, jj + 1)
                V.tensor_tensor(yb2[:], vs[:, :, ds(jj, 1)].rearrange("p h a -> p (h a)"), ps[:, 6, 304:312], ALU.mult)
                dve.drain()
                V.tensor_tensor(q[:, :, ds(NP + jj, 1)].rearrange("p h a -> p (h a)"), yb2[:], ps[:, 6, 288:296], ALU.add
                                ).then_inc(pvs_out, 1)
                taps(k1, W)
                dve.drain()
                V.scalar_tensor_tensor(conv[:, ds(jj, 1), 0:NP].rearrange("p a n -> p (a n)"), acc[:, 0, :], cwb[:, W:W + 1],
                                       acc[:, 1, :], ALU.add, ALU.add)
                dve.drain()
                V.tensor_tensor(ust[:], us[:], cwb[:, 0:W].unsqueeze(1).broadcast_to([P, NS, W]), ALU.mult)
                dve.drain()
                V.tensor_reduce(yb[:], ust[:], AX, ALU.add)
                dve.drain()
                V.tensor_scalar(conv[:, ds(jj, 1), NP:N].rearrange("p a n -> p (a n)"), yb[:], cwb[:, W:W + 1], None, ALU.add
                                ).then_inc(conv_done, 1)

            def conv_body(j):
                first = isinstance(j, int) and j == 0
                if not first:
                    lag_scores(j - 1)
                    taps(0, 10)
                    lag_softmax(j - 1)
                dve.wait_ge(s_mm, j + 1)
                if not first:
                    dve.wait_ge(pv_mm, j)
                where = [ps[:, 5, 384:512], ps[:, 7, 0:256], ps[:, 5, 0:384], ps[:, 4, :]]
                for t in range(QT):
                    lo, w = off[t], (t + 1) * P
                    V.scalar_tensor_tensor(pr[:, lo:lo + w], where[t], SCALE, sc[:, lo:lo + w], ALU.mult, ALU.add)
                dve.drain()
                for t in range(QT):
                    V.reduce_max(pm[:, t:t + 1], pr[:, off[t]:off[t] + (t + 1) * P], AX)
                dve.drain()
                V.tensor_scalar(pm[:, 4:8], pm[:, 0:4], -1.0, None, ALU.mult).then_inc(p_max, 1)
                if not first:
                    lag_weights(j - 1)
                    taps(10, 12)
                dve.wait_ge(p_exp, j + 1)
                V.reciprocal(pm[:, 12:16], pm[:, 8:12]).then_inc(p_inv, 1)
                if not first:
                    lag_rest(j - 1)
                dve.wait_ge(p_tr, j + 1)
                V.tensor_copy(us[:, :, 0:W - 1], ps[:, 6, 0:240].rearrange("p (b w) -> p b w", b=NS)).then_inc(us_stated, 1)
                dve.wait_ge(free_act, T_CONV - T_V + 2 * j + 2)
                V.tensor_tensor(u[:, W - 1:W - 1 + NP], ua[:, 0:NP], sg[:, 0:NP], ALU.mult)
                V.tensor_tensor(us[:, :, W - 1], ua[:, NP:N], sg[:, NP:N], ALU.mult).then_inc(u_ready, 1)
                dve.drain()
            loop(dve, CT, conv_body)
            lag_scores(7)
            lag_softmax(7)
            taps(0, 2)
            lag_weights(7)
            lag_rest(7, 2, 8)
            dve.drain()

            dve.wait_ge(p_tr, CT + 1)
            dve.wait_ge(mu_mm, 1)
            V.tensor_scalar(two(t1[:, 0, :]), ps[:, 6:8, 0:NH], 1.0 / C, None, ALU.mult)
            dve.drain()
            for c in range(CT):
                V.tensor_tensor(conv[:, c, :], conv[:, c, :], t1[:, 0, :], ALU.subtract).then_inc(csub, 1)
            inv_std(2, C)

            def c_low(c):
                dve.wait_ge(mhi, H + c + 1)
                V.tensor_tensor(a_lo[:, c, :], conv[:, c, :], a_hi[:, c, :].bitcast(F32), ALU.subtract).then_inc(mlo, 1)
            for c in range(CT):
                dve.wait_ge(csig_done, c + 1)
                V.tensor_tensor(conv[:, c, :], sq[:, c % 2, :], t1[:, c % 2, :], ALU.mult).then_inc(mix_done, 1)
                if c >= 1:
                    c_low(c - 1)
            c_low(CT - 1)

            def residual(units, m, gate, tp):
                dve.wait_ge(split_used, units)
                acc_p = pair(tp)
                xm = pick(xT, m)
                g0 = mod[:, ds(gate + m, 1), 0:1].rearrange("p a n -> p (a n)")
                gs = mod[:, ds(gate + m, 1), 1:9].rearrange("p a n -> p (a n)")
                V.scalar_tensor_tensor(xm[:, 0:NH], acc_p[:, 0, :], g0, xm[:, 0:NH], ALU.mult, ALU.add)
                V.scalar_tensor_tensor(xm[:, NH:NP], acc_p[:, 1, 0:NP - NH], g0, xm[:, NH:NP], ALU.mult, ALU.add)
                V.tensor_tensor(hs[:, tp, :], acc_p[:, 1, NP - NH:NH], gs, ALU.mult).then_inc(free_dve, 1)
                dve.drain()
                V.tensor_tensor(xm[:, NP:N], xm[:, NP:N], hs[:, tp, :], ALU.add).then_inc(x_updated, 1)

            dve.wait_ge(reloaded, 16)
            dve.drain()
            def ada_beside(i, e):
                for g in range(2):
                    n = 4 * (ADA_FIRST + i - 1) + 2 * e + g
                    dve.wait_ge(ada_hi_done, n + 1)
                    dve.wait_ge(ada_used, n - 1)
                    V.tensor_tensor(adl_lo[:, g, :], adl[:, g, :], adl_hi[:, g, :].bitcast(F32), ALU.subtract
                                    ).then_inc(ada_lo_done, 1)

            def out_body(i):
                for e in range(2):
                    if not isinstance(i, int) or i > 0:
                        ada_beside(i, e)
                    residual(4 * (T_OUT + 2 * i + e + 1), 2 * i + e, 32, (T_OUT + e) % 2)
                    if e == 1 and (not isinstance(i, int) or i > 1):
                        mods(ADA_FIRST + i - 2, 5)
            loop(dve, KT // 2, out_body, first=2)
            dve.drain()
            mods(ADA_FIRST + ADA_OUT - 1, 5)
            dve.drain()
            add_bias(4 * ADA_FIRST, 4 * (ADA_FIRST + ADA_OUT))
            gains(1)
            inv_std(3, D)
            normed(1, 48)
            for c in range(24 - ADA_GAP, 24):
                mods(c, 5)
            dve.drain()
            add_bias(96 - 4 * ADA_GAP, 96)

            def up(b, i):
                for e in range(2):
                    n = 2 * i + e
                    tp = (T_FF + e) % 2
                    dve.wait_ge(split_used, U_FF + b * U_BLOCK + 4 * (n + 1))
                    V.tensor_scalar(two(sq[:, e, :]), pair(tp), 0.0, None, ALU.max)
                    dve.drain()
                    V.tensor_tensor(two(t1[:, e, :]), two(sq[:, e, :]), pair(tp), ALU.mult).then_inc(hb_done, 1)
                    dve.wait_ge(bhi, b * FB + n + 1)
                    V.tensor_tensor(pick(b_lo, n), t1[:, e, :], pick(b_hi, n).bitcast(F32), ALU.subtract).then_inc(blo, 1)

            def down(b, i):
                for e in range(2):
                    residual(U_FF + b * U_BLOCK + 4 * FB + 2 * (2 * i + e + 1), 2 * i + e, 80, (T_FF + e) % 2)
            with dve.Fori(0, BLOCKS) as b:
                with dve.Fori(0, FB // 2) as i:
                    up(b, i)
                with dve.Fori(0, KT // 2) as i:
                    down(b, i)

            dve.wait_ge(g_in, 16)
            for t in range(QT + 1):
                n = P if t < QT else NS
                dve.wait_ge(f_sum, t + 1)
                V.tensor_scalar(fstat[0:n, t, 1:2], fstat[0:n, t, 0:1], 1.0 / D, EPS, ALU.mult, ALU.add).then_inc(f_var, 1)
                dve.wait_ge(f_std, t + 1)
                V.reciprocal(fstat[0:n, t, 3:4], fstat[0:n, t, 2:3])
                dve.drain()
                V.tensor_scalar(fstat[0:n, t, 4:5], fstat[0:n, t, 3:4], fstat[0:n, t, 3:4], -0.5, ALU.mult, ALU.mult)
                dve.drain()
                V.tensor_scalar(fstat[0:n, t, 4:5], fstat[0:n, t, 4:5], fstat[0:n, t, 1:2], 1.5, ALU.mult, ALU.add)
                dve.drain()
                V.tensor_scalar(fstat[0:n, t, 3:4], fstat[0:n, t, 3:4], fstat[0:n, t, 4:5], None, ALU.mult)
                dve.drain()
                if t >= 2:
                    dve.wait_ge(y_stored[t % 2], 16 * (t // 2))
                V.scalar_tensor_tensor(yrow[0:n, t % 2, :], ps[0:n, 4 * (t % 2):4 * (t % 2) + 4, :].rearrange("p a n -> p (a n)"),
                                       fstat[0:n, t, 3:4], grow[0:n, :], ALU.mult, ALU.mult).then_inc(f_y, 1)

        @block.tensor
        def _(pe):
            mm, tr = nc.tensor.matmul, nc.tensor.transpose

            def transpose(out, in_):
                n = in_.shape[0]
                return tr(out, in_, ident[0:n, 0:n])

            def by_product(out, in_):
                n = in_.shape[0]
                return mm(out, in_, ident[0:n, 0:n], start=True, stop=True)

            pe.wait_ge(ident_in, 16)
            pe.wait_ge(silu_done, 1)
            for kt in range(KT):
                last = transpose(ps[:, 0, kt * 9:kt * 9 + 9], csil[:, kt * P:(kt + 1) * P])
            last.then_inc(c_tr, 1)
            pe.wait_ge(vec_in, 16 * 7)
            transpose(ps[:, 1, 0:56], vrow[0:56, :])
            transpose(ps[:, 2, 0:96], brow[0:96, :])
            for c in range(CT):
                last = transpose(ps[:, 3, c * W:(c + 1) * W], cwrow[:, c * P:(c + 1) * P])
            last.then_inc(vec_tr, 1)
            for n in range(4 * QT):
                t, g = n // 4, n % 4
                if g == 0:
                    pe.wait_ge(x_in[t % 2], 16 * (t // 2 + 1))
                if n >= 4:
                    if n % 2:
                        pe.wait_ge(x_copied_act, (n - 4) // 2 + 1)
                    else:
                        pe.wait_ge(x_copied_dve, (n - 4) // 2 + 1)
                for f in range(4):
                    last = transpose(ps[:, 4 + n % 4, f * P:(f + 1) * P], xtok[:, t % 2, (4 * g + f) * P:(4 * g + f + 1) * P])
                last.then_inc(x_tr, 1)
            pe.wait_ge(xs_in, 16)
            pe.wait_ge(x_copied_dve, 7)
            for f in range(KT):
                last = transpose(ps[:, 4, f * NS:(f + 1) * NS], xrow[:, f * P:(f + 1) * P])
            last.then_inc(x_tr, 1)
            pe.wait_ge(ones_set, 1)

            def sum_squares(f, count, slot, n):
                pe.wait_ge(sq_done, n + 1)
                for h in range(2):
                    last = mm(ps[:, 6 + h, 0:NH], ones[:], sq[:, slot, h * NH:(h + 1) * NH], start=(f == 0), stop=(f == count - 1))
                last.then_inc(sq_summed, 1)
                return last

            def ada_group(bank, kt0, hi_, lo_):
                for kk in range(4):
                    for n, w in enumerate((hi_, lo_)):
                        last = mm(ps[0:18, bank, :], cT[:, kt0 + kk, :], w[:, kk * 512:(kk + 1) * 512],
                                  start=(kt0 + kk == 0 and n == 0), stop=(kt0 + kk == KT - 1 and n == 1))
                last.then_inc(ada_used, 1)

            def mod_tr(c, bank):
                pe.wait_ge(ada_row, c + 1)
                for f in range(4):
                    last = by_product(ps[:, bank, f * 18:f * 18 + 18], arow[:, f * P:(f + 1) * P])
                last.then_inc(ada_tr, 1)

            def ada_chunks(i, count=2):
                for e in range(count):
                    c = 2 * i + e
                    if not isinstance(i, int) or i > 0:
                        pe.wait_ge(ada_row, c - 1)
                    for g in range(4):
                        pe.wait_ge(ada_lo_done, 4 * c + g + 1)
                        ada_group(e, 4 * g, ada_hi[:, g, :], ada_lo[:, g % 2, :])
                        if isinstance(c, int) and c < 4:
                            sum_squares(4 * c + g, KT, g % 2, 4 * c + g)
                    if not isinstance(i, int) or c > 2:
                        pe.wait_ge(mod_done, c - 2)
                    if not isinstance(i, int) or c > 0:
                        mod_tr(c - 1, 3 - e)

            def ada_beside(i, e):
                if e == 0:
                    pe.wait_ge(ada_row, ADA_FIRST + i - 1)
                for g in range(2):
                    pe.wait_ge(ada_lo_done, 4 * (ADA_FIRST + i - 1) + 2 * e + g + 1)
                    ada_group(4, 8 * e + 4 * g, adl_hi[:, g, :], adl_lo[:, g, :])

            def late_tr(c):
                pe.wait_ge(mod_done, c)
                mod_tr(c, 5)

            pe.wait_ge(c_ready, 1)
            pe.wait_ge(vec_ready, 1)
            pe.wait_ge(x_copied_act, 8)
            pe.wait_ge(x_copied_dve, 9)
            ada_chunks(0)
            ada_chunks(1)
            ada_chunks(2)
            for n in range(NS):
                pe.wait_ge(kpair_ready, n + 1)
                if n >= 2:
                    pe.wait_ge((kis_dve, kis_act)[n % 2], n // 2)
                for key in range(4):
                    last = transpose(ps[:, 4 + n % 2, key * P:(key + 1) * P],
                                     kpair[:, n // 2, n % 2, key, :, :].rearrange("p e d -> p (e d)"))
                last.then_inc(kid_tr, 1)
            loop(pe, ADA_FIRST // 2 - 3, lambda i: ada_chunks(3 + i), first=0)
            ada_chunks(ADA_FIRST // 2, 1)
            pe.wait_ge(mod_done, ADA_FIRST - 2)
            mod_tr(ADA_FIRST - 1, 2)

            def halves(T, tp, gp, uu, kk, kt, x_hi, x_lo, start, stop, skip=0):
                whi, wlo = w_hi[:, 4 * gp + uu, kk, skip:P], w_lo[:, 4 * gp + uu, kk, skip:P]
                out = [ps[0:P - skip, 2 * tp + h, 0:NH] for h in range(2)]
                for w, x, first, end in ((whi, x_hi, start, False), (whi, x_lo, False, False), (wlo, x_hi, False, stop)):
                    for h in range(2):
                        last = mm(out[h], w, x[:, kt, h * NH:(h + 1) * NH], start=first, stop=end)
                return last

            def tile(T, tp, G, gp, free, mid=None, ada_part=None, skip=0, k0=0):
                if free is not None:
                    pe.wait_ge(*free)
                mids = mid if isinstance(mid, dict) else {2: mid}
                for uu in range(4):
                    if mids.get(uu) is not None:
                        mids[uu]()
                    if uu == 3 and ada_part is not None:
                        ada_part()
                    pe.wait_ge(lo_done, 4 * G + uu + 1)
                    for kk in range(4):
                        n = 4 * uu + kk
                        last = halves(T, tp, gp, uu, kk, (n + k0) % KT, a_hi, a_lo, n == 0, n == KT - 1, skip)
                    last.then_inc(split_used, 1)

            def pair_product(T, t, n, kk, k0):
                return halves(T + t, (T + t) % 2, (T + t) % 2, n // 4, kk, (n + k0) % KT, a_hi, a_lo, n == 0, n == KT - 1,
                              MISC_SKIP if T + t == T_MISC else 0)

            def two_tiles_begin(T, frees, ready, n0=0, n1=KT - KU, k0=0):
                for free in frees:
                    pe.wait_ge(*free)
                for n in range(n0, n1):
                    if n % 4 == 0:
                        pe.wait_ge(lo_done, 4 * (T + 1) + n // 4 + 1)
                    ready((n + k0) % KT)
                    for t in range(2):
                        pair_product(T, t, n, n % 4, k0)

            def two_tiles_end(T, ready, between=None, k0=0):
                if between is not None:
                    between(T)
                    between(T + 1)
                pe.wait_ge(lo_done, 4 * (T + 1) + 4)
                for t in range(2):
                    for n in range(KT - KU, KT):
                        if t == 0:
                            ready((n + k0) % KT)
                        last = pair_product(T, t, n, n % 4, k0)
                    last.then_inc(split_used, 1 if t else 7)

            def normed_ready(n):
                def ready(kt):
                    pe.wait_ge(nlo_done, (KT + 1) * n + kt + 2)
                return ready

            two_tiles_begin(T_MISC, [(mod_done, ADA_FIRST)], normed_ready(0))
            two_tiles_end(T_MISC, normed_ready(0))

            def misc_transposes():
                pe.wait_ge(wi_ready, 1)
                for t in range(QT):
                    transpose(ps[:, 4, t * HI:(t + 1) * HI], wiT[:, t * P:(t + 1) * P])
                transpose(ps[0:NS, 5, 0:HI], wiT[:, NP:N])
                pe.wait_ge(free_dve, T_MISC + 1)
                for t in range(QT):
                    transpose(ps[:, 6, t * DI:(t + 1) * DI], kiT[0:DI, t * P:(t + 1) * P])
                transpose(ps[0:NS, 7, 0:DI], kiT[0:DI, NP:N]).then_inc(mt_tr, 1)

            def index_products(m, k):
                if m == 0 and k == 0:
                    pe.wait_ge(ki_lo_done, 1)
                    pe.wait_ge(mt_act, 1)
                    pe.wait_ge(mt_dve, 1)
                pe.wait_ge(qi_lo_done, m + 1)
                for n in (6 * m + k, 6 * m + k + 1):
                    t, h = n % 3 + 1, n // 3
                    if n >= 2:
                        pe.wait_ge(isc_relu, n - 1)
                    w = qiw[m % 2][:, m // 2 * 2 + h % 2, (t - 1) * P:t * P]
                    mm(ps[:, 4 + n % 2, 0:(t + 1) * P], w, ki_hi[:, 0:(t + 1) * P], start=True, stop=False)
                    mm(ps[:, 4 + n % 2, 0:(t + 1) * P], w, ki_lo[:, 0:(t + 1) * P], start=False, stop=True).then_inc(isc_done, 1)

            def index_mids(m, two=lambda: None, three=lambda: None):
                return {1: lambda: index_products(m, 0), 2: lambda: (index_products(m, 2), two()),
                        3: lambda: (index_products(m, 4), three())}

            for m in range(1, HI // 2):
                T = T_QI + m
                tile(T, T % 2, T, T % 2, (free_dve, T - 1), mid=misc_transposes if m == 1 else index_mids(m - 2))

            def new_key():
                pe.wait_ge(pq_done, 1)
                mm(ps[0:NS, 6, 0:HI * NS], ones[0:DI, 0:NS], pq[0:DI, :, :].rearrange("p h b -> p (h b)"), start=True, stop=True
                   ).then_inc(nw_mm, 1)

            def q_body(i):
                for e in range(2):
                    b = 2 * i + e
                    T, tp = T_Q + b, (T_Q + e) % 2
                    first = isinstance(i, int) and b == 0

                    def dots():
                        pe.wait_ge(ident_in, 16)
                        if first:
                            pe.wait_ge(nw_done, 1)
                        pe.wait_ge(qisb_set, b + 1)
                        if not first:
                            pe.wait_ge(sadd, b)
                        mm(ps[0:HI, 6, 0:HI], qisb[:, e, :], ident[:, 0:HI], start=True, stop=True)
                        for c in range(2):
                            last = mm(ps[0:HI, 6 + c, :], qisb[:, e, :],
                                      kisT[:, ds(i, 1), c * 512:(c + 1) * 512].rearrange("p a n -> p (a n)"), start=True, stop=True)
                        last.then_inc(sdots, 1)
                    mid = dots
                    if isinstance(i, int) and i == 0:
                        mid = index_mids(7, three=dots) if e else index_mids(6, two=new_key, three=dots)
                    tile(T, tp, T, tp, (free_dve, T - 1), mid=mid)
                    pe.wait_ge(ident_in, 16)
                    pe.wait_ge(srelu, b + 1)
                    for c in range(2):
                        last = mm(ps[0:NS, 6 + c, :], wib[:], rsd[:, c, :], start=True, stop=True)
                    last.then_inc(ssum, 1)
            loop(pe, 4, q_body)

            def kv_transposes(n, slot_tp, ready):
                pe.wait_ge(*ready)
                if not isinstance(n, int) or n >= 1:
                    pe.wait_ge(kv_staged, n)
                for t in range(QT):
                    transpose(ps[:, 4, t * P:(t + 1) * P], kv[:, slot_tp, t * P:(t + 1) * P])
                transpose(ps[0:NS, 5, 0:P], kv[:, slot_tp, NP:N]).then_inc(kv_tr, 1)

            def k_body(i):
                for e in range(2):
                    n = 2 * i + e
                    T, tp = T_K + n, (T_K + e) % 2
                    first = isinstance(i, int) and n == 0
                    tile(T, tp, T, tp, (free_dve, T - 1),
                         mid=None if first else lambda: kv_transposes(n - 1, 1 - tp, (free_dve, T)))
            loop(pe, 4, k_body)

            def v_body(i):
                for e in range(2):
                    n = 2 * i + e
                    T, tp = T_V + n, (T_V + e) % 2
                    if isinstance(i, int):
                        free = (free_dve, T - 1)
                        ready = (free_dve, T_V) if n == 0 else (free_act, n)
                    else:
                        free, ready = (free_act, n - 1), (free_act, n)
                    tile(T, tp, T, tp, free, mid=lambda: kv_transposes(8 + n - 1, 1 - tp, ready))
            loop(pe, 4, v_body)

            p_at = [0, 512, 896, 1152]

            def broadcast_q(jj):
                pe.wait_ge(qsb_set, jj + 1)
                pe.wait_ge(pT_ready, jj + 1)
                if not isinstance(jj, int) or jj > 0:
                    pe.wait_ge(u_staged, jj)
                for h in range(H):
                    last = mm(ps[:, 4 + h // 4, h % 4 * P:(h % 4 + 1) * P], qsb[:, h:h + 1].broadcast_to([P, P]), ident[:],
                              start=True, stop=True)
                last.then_inc(qb_mm, 1)

            def weighted_v(jj):
                pe.wait_ge(vh_in, 16 * (jj + 1))
                pe.wait_ge(pT_ready, jj + 1)
                for s in range(QT):
                    last = mm(ps[:, 7, s * P:512], vh[:, s, :], pr[:, p_at[s]:p_at[s] + (QT - s) * P], start=(s == 0),
                              stop=(s == QT - 1))
                last.then_inc(pv_mm, 1)

            def row_scores(jj):
                pe.wait_ge(ident_in, 16)
                pe.wait_ge(km_done, jj + 1)
                pe.wait_ge(us_stated, jj + 1)
                if not isinstance(jj, int) or jj > 0:
                    pe.wait_ge(s_ready, jj)
                for t in range(2):
                    last = transpose(ps[0:H, 6, t * P:(t + 1) * P], sT[:, t, :])
                last.then_inc(sT_tr, 1)

            def row_weights(jj):
                pe.wait_ge(ident_in, 16)
                pe.wait_ge(s_ready, jj + 1)
                if not isinstance(jj, int) or jj > 0:
                    pe.wait_ge(pTs_ready, jj)
                for t in range(2):
                    last = transpose(ps[:, 6, 256 + t * H:256 + (t + 1) * H], sm[:, t * P:(t + 1) * P])
                last.then_inc(sp_tr, 1)

            def row_output(jj):
                pe.wait_ge(ident_in, 16)
                pe.wait_ge(pTs_ready, jj + 1)
                pe.wait_ge(vg_in, 32 * (jj + 1))
                if not isinstance(jj, int) or jj > 0:
                    pe.wait_ge(pvs_out, jj)
                for h in range(H):
                    for t in range(2):
                        mm(ps[:, 6, 288 + h:289 + h], vg[:, t, h * P:(h + 1) * P], pTs[:, t, h:h + 1], start=(t == 0), stop=(t == 1))
                mm(ps[:, 6, 304:312], ones[0:H, :], dg[:], start=True, stop=True).then_inc(pvs_mm, 1)

            def u_transposes(jj):
                pe.wait_ge(ident_in, 16)
                pe.wait_ge(u_ready, jj + 1)
                transpose(ps[0:W - 1, 7, 384:512], u[:, NP:NP + W - 1])
                return transpose(ps[0:NS, 5, 384:512], us[:, :, W - 1])

            def conv_body(j):
                first = isinstance(j, int) and j == 0
                Ta, pa = T_CONV + 2 * j, T_CONV % 2
                if first:
                    tile(Ta, pa, Ta, pa, (free_act, Ta - 1 - T_V), mid=lambda: kv_transposes(15, 0, (free_act, 8)))
                else:
                    tile(Ta, pa, Ta, pa, (free_act, Ta - 1 - T_V),
                         mid={1: lambda: broadcast_q(j - 1), 2: lambda: weighted_v(j - 1)})
                    row_scores(j - 1)
                if first:
                    pe.wait_ge(idx_ready, 1)
                    pe.wait_ge(kv_staged, 16)
                    for i, what in enumerate((1, 2)):
                        for t in range(2):
                            transpose(ps[:, 6, 16 * i + 8 * t:16 * i + 8 * t + 8], fi[:, what, t * P:(t + 1) * P])
                    for b in range(NS):
                        mm(ps[0:H, 6, 32 + b:33 + b], pq[:, 0:H, b], ones[:, 0:1], start=True, stop=True)
                    mm(ps[0:H, 6, 40:48], ssc[:, 0:1].broadcast_to([NS, H]), ident[0:NS, 0:NS], start=True, stop=True
                       ).then_inc(idx_tr, 1)
                pe.wait_ge(qh_set, j + 1)
                if not first:
                    pe.wait_ge(km_done, j)
                    pe.wait_ge(pv_out, j)
                where = [ps[:, 5, 384:512], ps[:, 7, 0:256], ps[:, 5, 0:384], ps[:, 4, :]]
                for t in range(QT):
                    last = mm(where[t], qh[:, t * P:(t + 1) * P], k[:, ds(j, 1), 0:(t + 1) * P].rearrange("p a n -> p (a n)"),
                              start=True, stop=True)
                last.then_inc(s_mm, 1)
                tile(Ta + 1, 1 - pa, Ta + 1, 1 - pa, (free_act, Ta - T_V),
                     mid=None if first else {2: lambda: row_weights(j - 1), 3: lambda: row_output(j - 1)})
                pe.wait_ge(ident_in, 16)
                pe.wait_ge(st_in, 16 * (j + 1))
                if first:
                    pe.wait_ge(snew_ready, 1)
                else:
                    pe.wait_ge(pvs_out, j)
                for g in range(2):
                    transpose(ps[:, 6, 120 * g:120 * (g + 1)], st[:, g, :])
                pe.wait_ge(p_ready, j + 1)
                if not first:
                    u_transposes(j - 1)
                for s in range(QT):
                    for t in range(s, QT):
                        at_ = t * (t + 1) // 2 * P + s * P
                        out = {0: (4, 0), 1: (5, 0), 2: (7, 0), 3: (7, 256)}[s]
                        last = transpose(ps[:, out[0], out[1] + (t - s) * P:out[1] + (t - s + 1) * P], pr[:, at_:at_ + P])
                last.then_inc(p_tr, 1)
            loop(pe, CT, conv_body)
            broadcast_q(7)
            weighted_v(7)
            row_scores(7)
            row_weights(7)
            row_output(7)
            pe.wait_ge(pv_out, 8)
            pe.wait_ge(km_done, 8)
            u_transposes(7).then_inc(p_tr, 1)

            pe.wait_ge(pvs_out, NS)
            pe.wait_ge(u_staged, CT)

            def channel_sum(c):
                pe.wait_ge(conv_done, c + 1)
                for h in range(2):
                    last = mm(ps[:, 6 + h, 0:NH], ones[:], conv[:, c, h * NH:(h + 1) * NH], start=(c == 0), stop=(c == CT - 1))
                return last
            for c in range(CT - 1):
                channel_sum(c)
            def mixed(kt):
                pe.wait_ge(*((qlo, kt - CT + 1) if kt >= CT else (mlo, kt + 1)))
            two_tiles_begin(T_OUT, [(free_act, T_OUT - T_V)], mixed, 0, CT, k0=CT)

            last = channel_sum(CT - 1)
            last.then_inc(mu_mm, 1)
            for c in range(CT):
                if c == 0:
                    pe.wait_ge(csub, 1)
                sum_squares(c, CT, c % 2, KT + c)

            two_tiles_begin(T_OUT, [], mixed, CT, KT - KU, k0=CT)
            two_tiles_end(T_OUT, mixed, k0=CT)

            def sum_squares_of(m, slot):
                pe.wait_ge(sq_done, KT + CT + m + 1)
                for h in range(2):
                    last = mm(ps[:, 6 + h, 0:NH], ones[:], sq[:, slot, h * NH:(h + 1) * NH],
                              start=isinstance(m, int) and m == 0, stop=isinstance(m, int) and m == KT - 1, skip_group_check=True)
                last.then_inc(sq_summed, 1)

            def out_body(i):
                for e in range(2):
                    m = 2 * i + e
                    T, tp = T_OUT + m, (T_OUT + e) % 2

                    def last_squares():
                        sum_squares_of(m - 2, e)
                        if e == 1 and (not isinstance(i, int) or i > 1):
                            late_tr(ADA_FIRST + i - 2)
                    tile(T, tp, T, tp, (free_dve, T_V + m - 1), mid=last_squares,
                         ada_part=lambda: ada_beside(i, e), k0=CT)
            out_body(1)
            with pe.Fori(2, KT // 2) as i:
                out_body(i)
            sum_squares_of(KT - 2, 0)
            sum_squares_of(KT - 1, 1)
            late_tr(23 - ADA_GAP)
            for c in range(24 - ADA_GAP, 24):
                if c == 23:
                    pe.wait_ge(var_done, 3)
                for g in range(4):
                    n = 2 * ADA_OUT + 2 * (c - 24 + ADA_GAP) + g // 2
                    pe.wait_ge(adl_landed[g % 2], 16 * (n + 1))
                    for kk in range(4):
                        last = mm(ps[0:18, 4 + 2 * (c - 22), :], cT[:, 4 * g + kk, :].bitcast(F32),
                                  adl[:, g % 2, kk * 512:(kk + 1) * 512], start=(g == 0 and kk == 0), stop=(g == 3 and kk == 3))
                    last.then_inc(ada_used, 1)

            def half_tile(T, tp, G, gp, u0, free, ready=None):
                pe.wait_ge(*free)
                for uu in (u0, u0 + 1):
                    pe.wait_ge(lo_done, 4 * G + uu + 1)
                    for kk in range(4):
                        kt = 4 * (uu - u0) + kk
                        if ready is not None:
                            ready(kt)
                        last = halves(T, tp, gp, uu, kk, kt, b_hi, b_lo, kt == 0, kt == FB - 1)
                    last.then_inc(split_used, 1)

            D0 = T_V + KT

            def block_body(b):
                first = isinstance(b, int)
                if first:
                    two_tiles_begin(T_FF, [(free_dve, D0)], normed_ready(1))
                    two_tiles_end(T_FF, normed_ready(1), lambda T: late_tr(22 + T - T_FF))
                else:
                    for n in range(2):
                        G, par = T_FF + b * 16 + n, (T_FF + n) % 2
                        tile(G, par, G, par, (free_dve, D0 + b * KT - 1 + n))
                with pe.Fori(1, FB // 2) as i:
                    for e in range(2):
                        G, par = T_FF + b * 16 + 2 * i + e, (T_FF + e) % 2
                        tile(G, par, G, par, (hb_done, b * FB + 2 * i + e - 1))

                def down(i):
                    for e in range(2):
                        G, gp = T_FF + b * 16 + FB + 2 * i + e, (T_FF + e) % 2
                        for half in range(2):
                            m = 4 * i + 2 * e + half
                            if isinstance(i, int) and m < 2:
                                free = (hb_done, b * FB + FB - 1 + m)
                            else:
                                free = (free_dve, D0 + b * KT + m - 1)
                            half_tile(None, (T_FF + half) % 2, G, gp, 2 * half, free,
                                      (lambda kt: pe.wait_ge(blo, b * FB + kt + 1)) if isinstance(i, int) and m == 0 else None)
                loop(pe, KT // 4, down)
            block_body(0)
            with pe.Fori(1, BLOCKS) as b:
                block_body(b)

            for t in range(QT + 1):
                n = P if t < QT else NS
                if t == 0:
                    pe.wait_ge(x_updated, KT * (1 + BLOCKS))
                if t >= 2:
                    pe.wait_ge(f_y, t - 1)
                for f in range(KT):
                    last = transpose(ps[0:n, 4 * (t % 2) + f // 4, f % 4 * P:(f % 4 + 1) * P], xT[:, f, t * P:t * P + n])
                last.then_inc(f_tr, 1)


_OUTS = [("y_prompt", (1, NP, D)), ("y_sample", (NS, 1, D)), ("k_prompt", (1, 1, NP, H, P)), ("v_prompt", (1, 1, NP, H, P)),
         ("kidx_prompt", (1, 1, NP, DI)), ("conv_prompt", (1, 1, W - 1, C)), ("k_sample", (1, NS, 1, H, P)),
         ("v_sample", (1, NS, 1, H, P)), ("kidx_sample", (1, NS, 1, DI)), ("conv_sample", (1, NS, W - 1, C))]


def constants():
    import numpy as np

    pos = np.concatenate([np.arange(NP), np.full(NS, PAST)]).astype(np.float32)
    out = {}
    for name, width in (("", P), ("i", DI)):
        half = width // 2
        inv = (10000.0 ** (-np.arange(half) / half)).astype(np.float32)
        ang = (pos[None, :] * inv[:, None]).astype(np.float32)
        cos, sin = np.cos(ang).astype(np.float32), np.sin(ang).astype(np.float32)
        out[f"const_{name}cos"] = np.tile(np.concatenate([cos, cos]), (P // width, 1))
        out[f"const_{name}sin"] = np.tile(np.concatenate([-sin, sin]), (P // width, 1))
    out["const_ident"] = np.eye(P, dtype=np.float32)
    q_, s_ = np.arange(P)[:, None], np.arange(P)[None, :]
    out["const_future"] = np.where(s_ > q_, np.float32(FUTURE), np.float32(0.0)).astype(np.float32)
    out["const_onehot"] = np.ascontiguousarray(np.broadcast_to(np.eye(NS, dtype=np.float32), (HI, NS, NS)))
    return out


def kernel(**inputs):
    import numpy as np
    import concourse.bacc as bacc
    from concourse.bass_utils import run_bass_kernel_spmd

    nc = bacc.Bacc("TRN2", target_bir_lowering=False, num_devices=1)
    arrays, a, o = {}, {}, {}
    for name, value in list(inputs.items()) + list(constants().items()):
        value = np.ascontiguousarray(value)
        arrays[f"in_{name}"] = value
        a[name] = nc.dram_tensor(f"in_{name}", value.shape, mybir.dt.from_np(value.dtype), kind="ExternalInput").ap()
    for name, shape in _OUTS:
        o[name] = nc.dram_tensor(f"out_{name}", shape, F32, kind="ExternalOutput").ap()
    build(nc, a, o)
    r = run_bass_kernel_spmd(nc, [arrays], core_ids=[0])
    return tuple(r.results[0][f"out_{name}"] for name, _ in _OUTS)
```
